# Optimizing a Trainium2 kernel written in Bass

```python
import jax, jax.numpy as jnp
from jax import lax
import numpy as np
import jax
import jax.numpy as jnp

D_MODEL = 1024
BATCH = 1
SEQ = 256
DEPTH = 2

N_A_LAYERS = DEPTH // 2
N_B_LAYERS = DEPTH - N_A_LAYERS
CONV_WIDTH = 3
D_FF = 2816
N_HEADS = 8
QK_NOPE_DIM = 128
QK_ROPE_DIM = 64
V_HEAD_DIM = 128
Q_LORA_RANK = 512
KV_LORA_RANK = 256
ROPE_THETA = 10000.0
RMS_EPS = 1e-6
Q_BLOCK = 128


def rms_norm(x, g):
    xf = x.astype(jnp.float32)
    y = xf * lax.rsqrt(jnp.mean(xf * xf, axis=-1, keepdims=True) + RMS_EPS)
    return (y * g.astype(jnp.float32)).astype(x.dtype)

def causal_dwconv(x, w):
    c = x.shape[-1]
    return lax.conv_general_dilated(
        x, w[:, None, :].astype(x.dtype), window_strides=(1,),
        padding=((CONV_WIDTH - 1, 0),), dimension_numbers=("NWC", "WIO", "NWC"),
        feature_group_count=c)

def rope_tables(seq, dtype):
    inv = 1.0 / (ROPE_THETA ** (jnp.arange(0, QK_ROPE_DIM, 2, dtype=jnp.float32) / QK_ROPE_DIM))
    ang = jnp.arange(seq, dtype=jnp.float32)[:, None] * inv[None, :]
    return jnp.cos(ang).astype(dtype), jnp.sin(ang).astype(dtype)

def apply_rope(x, cos, sin):
    x1, x2 = jnp.split(x, 2, axis=-1)
    return jnp.concatenate([x1 * cos - x2 * sin, x1 * sin + x2 * cos], axis=-1)

def short_conv_mixer(x_n, w_in, conv_w, w_out):
    b, c, h = jnp.split(x_n @ w_in, 3, axis=-1)
    return (b * causal_dwconv(c * h, conv_w)) @ w_out

def conv_ffn(x_n, w_up, conv_w, w_down):
    g, u = jnp.split(causal_dwconv(x_n @ w_up, conv_w), 2, axis=-1)
    return (jax.nn.silu(g) * u) @ w_down

def shared_latent_kv(h, kv_in_norm, w_dkv, kv_norm, w_ukv, cos, sin):
    bsz, seq, _ = h.shape
    ckv = rms_norm(h, kv_in_norm) @ w_dkv
    c_kv, k_rope = ckv[..., :KV_LORA_RANK], ckv[..., KV_LORA_RANK:]
    k_rope = apply_rope(k_rope, cos, sin)
    kv = (rms_norm(c_kv, kv_norm) @ w_ukv).reshape(bsz, seq, N_HEADS, QK_NOPE_DIM + V_HEAD_DIM)
    return kv[..., :QK_NOPE_DIM], kv[..., QK_NOPE_DIM:], k_rope

def mla_attention(x_n, w_dq, q_norm, w_uq, w_o, k_nope, v, k_rope, cos, sin):
    bsz, seq, _ = x_n.shape
    q = (rms_norm(x_n @ w_dq, q_norm) @ w_uq).reshape(bsz, seq, N_HEADS, QK_NOPE_DIM + QK_ROPE_DIM)
    q_nope = q[..., :QK_NOPE_DIM]
    q_rope = apply_rope(q[..., QK_NOPE_DIM:], cos[:, None, :], sin[:, None, :])
    n_blk = seq // Q_BLOCK

    def to_blocks(t):
        return jnp.moveaxis(t.reshape(bsz, n_blk, Q_BLOCK, *t.shape[2:]), 1, 0)

    k_pos = jnp.arange(seq)
    scale = (QK_NOPE_DIM + QK_ROPE_DIM) ** -0.5

    def attend_block(args):
        qn, qr, blk = args
        s = (jnp.einsum('bqhd,bkhd->bhqk', qn, k_nope)
             + jnp.einsum('bqhr,bkr->bhqk', qr, k_rope)).astype(jnp.float32) * scale
        q_pos = blk * Q_BLOCK + jnp.arange(Q_BLOCK)
        s = jnp.where(k_pos[None, :] <= q_pos[:, None], s, -jnp.inf)
        p = jax.nn.softmax(s, axis=-1).astype(v.dtype)
        return jnp.einsum('bhqk,bkhd->bqhd', p, v)

    o = lax.map(attend_block, (to_blocks(q_nope), to_blocks(q_rope), jnp.arange(n_blk)))
    o = jnp.moveaxis(o, 0, 1).reshape(bsz, seq, N_HEADS * V_HEAD_DIM)
    return o @ w_o

def first_inputs(seed: int = 0) -> dict:
    key = jax.random.key(seed)
    ks = jax.random.split(key, 24)
    f32 = jnp.float32

    def w(k, shape, fan_in):
        return jax.random.normal(k, shape, f32) * (fan_in ** -0.5)

    def gain(k, shape):
        return 1.0 + 0.02 * jax.random.normal(k, shape, f32)

    return {
        "x": jax.random.normal(ks[0], (BATCH, SEQ, D_MODEL), f32),
        "a_mix_norm": gain(ks[1], (N_A_LAYERS, D_MODEL)),
        "a_w_in": w(ks[2], (N_A_LAYERS, D_MODEL, 3 * D_MODEL), D_MODEL),
        "a_conv": w(ks[3], (N_A_LAYERS, CONV_WIDTH, D_MODEL), CONV_WIDTH),
        "a_w_out": w(ks[4], (N_A_LAYERS, D_MODEL, D_MODEL), D_MODEL),
        "b_mix_norm": gain(ks[5], (N_B_LAYERS, D_MODEL)),
        "b_w_dq": w(ks[6], (N_B_LAYERS, D_MODEL, Q_LORA_RANK), D_MODEL),
        "b_q_norm": gain(ks[7], (N_B_LAYERS, Q_LORA_RANK)),
        "b_w_uq": w(ks[8], (N_B_LAYERS, Q_LORA_RANK, N_HEADS * (QK_NOPE_DIM + QK_ROPE_DIM)), Q_LORA_RANK),
        "b_w_o": w(ks[9], (N_B_LAYERS, N_HEADS * V_HEAD_DIM, D_MODEL), N_HEADS * V_HEAD_DIM),
        "kv_in_norm": gain(ks[10], (D_MODEL,)),
        "w_dkv": w(ks[11], (D_MODEL, KV_LORA_RANK + QK_ROPE_DIM), D_MODEL),
        "kv_norm": gain(ks[12], (KV_LORA_RANK,)),
        "w_ukv": w(ks[13], (KV_LORA_RANK, N_HEADS * (QK_NOPE_DIM + V_HEAD_DIM)), KV_LORA_RANK),
        "ffn_norm": gain(ks[14], (DEPTH, D_MODEL)),
        "ffn_w_up": w(ks[15], (DEPTH, D_MODEL, 2 * D_FF), D_MODEL),
        "ffn_conv": w(ks[16], (DEPTH, CONV_WIDTH, 2 * D_FF), CONV_WIDTH),
        "ffn_w_down": w(ks[17], (DEPTH, D_FF, D_MODEL), D_FF),
        "final_norm": gain(ks[18], (D_MODEL,)),
    }

def first_block(x, a_mix_norm, a_w_in, a_conv, a_w_out, b_mix_norm, b_w_dq, b_q_norm, b_w_uq, b_w_o,
              kv_in_norm, w_dkv, kv_norm, w_ukv, ffn_norm, ffn_w_up, ffn_conv, ffn_w_down, final_norm):
    cos, sin = rope_tables(x.shape[1], x.dtype)
    h = x
    shared = None
    for layer in range(DEPTH):
        if layer < N_A_LAYERS:
            h = h + short_conv_mixer(rms_norm(h, a_mix_norm[layer]), a_w_in[layer],
                                     a_conv[layer], a_w_out[layer])
        else:
            j = layer - N_A_LAYERS
            k_nope, v, k_rope = shared
            h = h + mla_attention(rms_norm(h, b_mix_norm[j]), b_w_dq[j], b_q_norm[j], b_w_uq[j],
                                  b_w_o[j], k_nope, v, k_rope, cos, sin)
        h = h + conv_ffn(rms_norm(h, ffn_norm[layer]), ffn_w_up[layer], ffn_conv[layer], ffn_w_down[layer])
        if layer == N_A_LAYERS - 1:
            shared = shared_latent_kv(h, kv_in_norm, w_dkv, kv_norm, w_ukv, cos, sin)
    return rms_norm(h, final_norm)


DEPTH_2 = 1

GRID_W = 64
CTX_LEN = 256
N_MIXERS = 3
EPS = 1e-6
D_FF_2 = 4 * D_MODEL
N_DIRS = 2

GLA_HEADS = 4
GLA_DK = D_MODEL // 2
GLA_DV = D_MODEL
GLA_HK = GLA_DK // GLA_HEADS
GLA_HV = GLA_DV // GLA_HEADS
GLA_IN = 2 * GLA_DK + 2 * GLA_DV
GLA_GATE_RANK = 16
GLA_TAU = 16.0
GLA_CHUNK = 64

MLSTM_HEADS = 4
MLSTM_INNER = 2 * D_MODEL
MLSTM_HD = MLSTM_INNER // MLSTM_HEADS
MLSTM_QKV_BLOCK = 4
MLSTM_N_BLOCKS = MLSTM_INNER // MLSTM_QKV_BLOCK
MLSTM_CONV = 4
MLSTM_CHUNK = 64

POOL_WINDOWS = (2, 4, 8, 16)
POOL_GROUP = D_MODEL // len(POOL_WINDOWS)


def rmsnorm(x, g):
    xf = x.astype(jnp.float32)
    y = xf * lax.rsqrt(jnp.mean(xf * xf, axis=-1, keepdims=True) + EPS)
    return (y * g.astype(jnp.float32)).astype(x.dtype)

def modulate(h, shift, scale):
    return h * (1 + scale) + shift

def head_rmsnorm(o, g):
    return o * lax.rsqrt(jnp.mean(o * o, axis=-1, keepdims=True) + EPS) * g.astype(jnp.float32)

def head_layernorm(o, g):
    mu = jnp.mean(o, axis=-1, keepdims=True)
    oc = o - mu
    return oc * lax.rsqrt(jnp.mean(oc * oc, axis=-1, keepdims=True) + EPS) * g.astype(jnp.float32)

def to_chunks(t, size):
    b, n = t.shape[0], t.shape[1] // size
    t = t.reshape((b, n, size) + t.shape[2:])
    return t.transpose((1, 0, 3, 2) + tuple(range(4, t.ndim)))

def from_chunks(t):
    n, b, h, c, d = t.shape
    return t.transpose(1, 0, 3, 2, 4).reshape(b, n * c, h, d)

def gla_chunk_scan(q, k, v, log_a, s0):
    f32 = jnp.float32
    qc, kc, vc, gc = (to_chunks(t.astype(f32), GLA_CHUNK) for t in (q, k, v, log_a))
    tri = jnp.tril(jnp.ones((GLA_CHUNK, GLA_CHUNK), dtype=bool))

    def step(s, blk):
        qb, kb, vb, gb = blk
        b = jnp.cumsum(gb, axis=2)
        b_last = b[:, :, -1:, :]
        q_dec = qb * jnp.exp(b)
        att = jnp.where(tri, jnp.einsum('bhtd,bhsd->bhts', q_dec, kb * jnp.exp(-b)), 0.0)
        o = jnp.einsum('bhts,bhsv->bhtv', att, vb) + jnp.einsum('bhtd,bhdv->bhtv', q_dec, s)
        s_new = (jnp.exp(b_last[:, :, 0, :])[..., None] * s
                 + jnp.einsum('bhsd,bhsv->bhdv', kb * jnp.exp(b_last - b), vb))
        return s_new, o

    s_fin, o = lax.scan(step, s0, (qc, kc, vc, gc))
    return from_chunks(o), s_fin

def mlstm_chunk_scan(q, k, v, log_i, log_f, state):
    f32 = jnp.float32
    qc, kc, vc = (to_chunks(t.astype(f32), MLSTM_CHUNK) for t in (q, k, v))
    ic, fc = (to_chunks(t.astype(f32), MLSTM_CHUNK) for t in (log_i, log_f))
    tri = jnp.tril(jnp.ones((MLSTM_CHUNK, MLSTM_CHUNK), dtype=bool))

    def step(carry, blk):
        c_bar, n_bar, m_prev = carry
        qb, kb, vb, ib, fb = blk
        b = jnp.cumsum(fb, axis=-1)
        d_mat = jnp.where(tri, b[..., :, None] - b[..., None, :] + ib[..., None, :], -jnp.inf)
        inter = b + m_prev[..., None]
        m_row = jnp.maximum(jnp.max(d_mat, axis=-1), inter)
        w_qk = jnp.einsum('bhtd,bhsd->bhts', qb, kb) * jnp.exp(d_mat - m_row[..., None])
        w_inter = jnp.exp(inter - m_row)
        num = (jnp.einsum('bhts,bhsv->bhtv', w_qk, vb)
               + w_inter[..., None] * jnp.einsum('bhtd,bhdv->bhtv', qb, c_bar))
        den = jnp.sum(w_qk, axis=-1) + w_inter * jnp.einsum('bhtd,bhd->bht', qb, n_bar)
        h = num / jnp.maximum(jnp.abs(den), jnp.exp(-m_row))[..., None]
        carry_log = b[..., -1] + m_prev
        tok_log = b[..., -1:] - b + ib
        m_new = jnp.maximum(carry_log, jnp.max(tok_log, axis=-1))
        w_tok = jnp.exp(tok_log - m_new[..., None])
        w_carry = jnp.exp(carry_log - m_new)
        k_w = kb * w_tok[..., None]
        c_new = w_carry[..., None, None] * c_bar + jnp.einsum('bhsd,bhsv->bhdv', k_w, vb)
        n_new = w_carry[..., None] * n_bar + jnp.sum(k_w, axis=2)
        return (c_new, n_new, m_new), h

    state_fin, h = lax.scan(step, state, (qc, kc, vc, ic, fc))
    return from_chunks(h), state_fin

def bidirectional_scan(scan_fn, ctx_dirs, lat_dirs, init):
    rev = lambda t: jnp.flip(t, axis=1)
    out_ctx, out_lat = [], []
    for direction in range(N_DIRS):
        ca, la = ctx_dirs[direction], lat_dirs[direction]
        if direction == 1:
            ca = tuple(rev(t) for t in ca)
            la = tuple(rev(t) for t in la)
        o_c, state = scan_fn(*ca, init)
        o_l, _ = scan_fn(*la, state)
        if direction == 1:
            o_c, o_l = rev(o_c), rev(o_l)
        out_ctx.append(o_c)
        out_lat.append(o_l)
    return out_ctx[0] + out_ctx[1], out_lat[0] + out_lat[1]

def gla_mixer(a_ctx, a_lat, w_in, w_a1, w_a2, b_a, g_head, w_o, need_ctx):
    def project(a):
        B, T, _ = a.shape
        q, k, v, r = jnp.split(a @ w_in, [GLA_DK, 2 * GLA_DK, 2 * GLA_DK + GLA_DV], axis=-1)
        q = q.reshape(B, T, GLA_HEADS, GLA_HK) * GLA_HK ** -0.5
        k = k.reshape(B, T, GLA_HEADS, GLA_HK)
        v = v.reshape(B, T, GLA_HEADS, GLA_HV)
        dirs = []
        for d in range(N_DIRS):
            z = (a @ w_a1[d]) @ w_a2[d] + b_a[d]
            log_a = jax.nn.log_sigmoid(z.astype(jnp.float32)) / GLA_TAU
            dirs.append((q, k, v, log_a.reshape(B, T, GLA_HEADS, GLA_HK)))
        return dirs, r

    def finish(o, r):
        B, T = o.shape[:2]
        o = head_rmsnorm(o, g_head).reshape(B, T, GLA_DV).astype(r.dtype)
        return (o * jax.nn.silu(r)) @ w_o

    ctx_dirs, r_ctx = project(a_ctx)
    lat_dirs, r_lat = project(a_lat)
    s0 = jnp.zeros((a_lat.shape[0], GLA_HEADS, GLA_HK, GLA_HV), jnp.float32)
    o_ctx, o_lat = bidirectional_scan(gla_chunk_scan, ctx_dirs, lat_dirs, s0)
    out_ctx = finish(o_ctx, r_ctx) if need_ctx else None
    return out_ctx, finish(o_lat, r_lat)

def centred_conv(x, w, b):
    K = w.shape[0]
    y = lax.conv_general_dilated(x, w[:, None, :], window_strides=(1,),
                                 padding=[(K // 2, K - 1 - K // 2)],
                                 dimension_numbers=('NWC', 'WIO', 'NWC'),
                                 feature_group_count=x.shape[-1])
    return y + b

def headwise(t, w):
    B, T, _ = t.shape
    t = t.reshape(B, T, MLSTM_N_BLOCKS, MLSTM_QKV_BLOCK)
    return jnp.einsum('btni,nij->btnj', t, w).reshape(B, T, MLSTM_INNER)

def mlstm_mixer(a_ctx, a_lat, w_up, conv_w, conv_b, w_qkv, w_gate, b_gate, g_norm, skip, w_down, need_ctx):
    H = MLSTM_HEADS

    def project(a):
        B, T, _ = a.shape
        xm, z = jnp.split(a @ w_up, 2, axis=-1)
        xc = jax.nn.silu(centred_conv(xm, conv_w, conv_b))
        q = headwise(xc, w_qkv[0])
        k = headwise(xc, w_qkv[1])
        v = headwise(xm, w_qkv[2])
        gin = jnp.concatenate([q, k, v], axis=-1)
        heads = lambda t: t.reshape(B, T, H, MLSTM_HD)
        qh, kh, vh = heads(q), heads(k) * MLSTM_HD ** -0.5, heads(v)
        dirs = []
        for d in range(N_DIRS):
            g = (gin @ w_gate[d] + b_gate[d]).astype(jnp.float32)
            dirs.append((qh, kh, vh, g[..., :H], jax.nn.log_sigmoid(g[..., H:])))
        return dirs, xc, z

    def finish(h, xc, z):
        B, T = h.shape[:2]
        hn = head_layernorm(h, g_norm).reshape(B, T, MLSTM_INNER).astype(xc.dtype)
        return ((hn + skip * xc) * jax.nn.silu(z)) @ w_down

    ctx_dirs, xc_ctx, z_ctx = project(a_ctx)
    lat_dirs, xc_lat, z_lat = project(a_lat)
    B = a_lat.shape[0]
    init = (jnp.zeros((B, H, MLSTM_HD, MLSTM_HD), jnp.float32),
            jnp.zeros((B, H, MLSTM_HD), jnp.float32),
            jnp.zeros((B, H), jnp.float32))
    h_ctx, h_lat = bidirectional_scan(mlstm_chunk_scan, ctx_dirs, lat_dirs, init)
    out_ctx = finish(h_ctx, xc_ctx, z_ctx) if need_ctx else None
    return out_ctx, finish(h_lat, xc_lat, z_lat)

def box_mean(x, axis, window):
    length = x.shape[axis]
    pad = [(0, 0)] * x.ndim
    pad[axis] = (1, 0)
    cs = jnp.pad(jnp.cumsum(x.astype(jnp.float32), axis=axis), pad)
    pos = jnp.arange(length)
    lo = jnp.maximum(pos - window // 2, 0)
    hi = jnp.minimum(pos + (window - window // 2), length)
    total = jnp.take(cs, hi, axis=axis) - jnp.take(cs, lo, axis=axis)
    shape = [1] * x.ndim
    shape[axis] = length
    return total / (hi - lo).astype(jnp.float32).reshape(shape)

def pool_mixer(a_ctx, a_lat, w_pool, b_pool, scale, need_ctx):
    B, T, D = a_lat.shape
    rows = T // GRID_W
    grid = a_lat.reshape(B, rows, GRID_W, D)
    lat_parts, ctx_parts = [], []
    for g, win in enumerate(POOL_WINDOWS):
        sl = slice(g * POOL_GROUP, (g + 1) * POOL_GROUP)
        hg = grid[..., sl]
        pooled = box_mean(box_mean(hg, 2, win), 1, win).astype(hg.dtype) - hg
        lat_parts.append(pooled.reshape(B, T, POOL_GROUP) @ w_pool[g] + b_pool[g])
        if need_ctx:
            cg = a_ctx[..., sl]
            pooled_c = box_mean(cg, 1, win).astype(cg.dtype) - cg
            ctx_parts.append(pooled_c @ w_pool[g] + b_pool[g])
    out_lat = jnp.concatenate(lat_parts, axis=-1) * scale
    out_ctx = jnp.concatenate(ctx_parts, axis=-1) * scale if need_ctx else None
    return out_ctx, out_lat

def sqrelu_mlp(h, w1, w2):
    return jnp.square(jax.nn.relu(h @ w1)) @ w2

def second_inputs(seed: int = 0) -> dict:
    key = jax.random.key(seed)
    keys = iter(jax.random.split(key, 48))

    def normal(shape, scale):
        return jax.random.normal(next(keys), shape, jnp.float32) * scale

    def gain(shape):
        return 1.0 + normal(shape, 0.02)

    n_gla = sum(1 for i in range(DEPTH_2) if i % N_MIXERS == 0)
    n_mlstm = sum(1 for i in range(DEPTH_2) if i % N_MIXERS == 1)
    n_pool = sum(1 for i in range(DEPTH_2) if i % N_MIXERS == 2)
    d = D_MODEL
    gate_i = normal((n_mlstm, N_DIRS, MLSTM_HEADS), 0.1)
    gate_f = jnp.linspace(3.0, 6.0, MLSTM_HEADS, dtype=jnp.float32) + normal((n_mlstm, N_DIRS, MLSTM_HEADS), 0.1)
    return {
        'x': normal((BATCH, SEQ, d), 1.0),
        'c': normal((BATCH, d), 1.0),
        'ctx': normal((BATCH, CTX_LEN, d), 1.0),
        'c_ctx': normal((d,), 1.0),
        'ada_w': normal((DEPTH_2, d, 6 * d), 0.5 * d ** -0.5),
        'ada_b': normal((DEPTH_2, 6 * d), 0.01),
        'norm1_g': gain((DEPTH_2, d)),
        'norm2_g': gain((DEPTH_2, d)),
        'mlp_w1': normal((DEPTH_2, d, D_FF_2), d ** -0.5),
        'mlp_w2': normal((DEPTH_2, D_FF_2, d), D_FF_2 ** -0.5),
        'gla_w_in': normal((n_gla, d, GLA_IN), d ** -0.5),
        'gla_w_a1': normal((n_gla, N_DIRS, d, GLA_GATE_RANK), d ** -0.5),
        'gla_w_a2': normal((n_gla, N_DIRS, GLA_GATE_RANK, GLA_DK), GLA_GATE_RANK ** -0.5),
        'gla_b_a': normal((n_gla, N_DIRS, GLA_DK), 0.1),
        'gla_g_head': gain((n_gla, GLA_HEADS, GLA_HV)),
        'gla_w_o': normal((n_gla, GLA_DV, d), GLA_DV ** -0.5),
        'mlstm_w_up': normal((n_mlstm, d, 2 * MLSTM_INNER), d ** -0.5),
        'mlstm_conv_w': normal((n_mlstm, MLSTM_CONV, MLSTM_INNER), MLSTM_CONV ** -0.5),
        'mlstm_conv_b': normal((n_mlstm, MLSTM_INNER), 0.01),
        'mlstm_w_qkv': normal((n_mlstm, 3, MLSTM_N_BLOCKS, MLSTM_QKV_BLOCK, MLSTM_QKV_BLOCK), MLSTM_QKV_BLOCK ** -0.5),
        'mlstm_w_gate': normal((n_mlstm, N_DIRS, 3 * MLSTM_INNER, 2 * MLSTM_HEADS), (3 * MLSTM_INNER) ** -0.5),
        'mlstm_b_gate': jnp.concatenate([gate_i, gate_f], axis=-1),
        'mlstm_g_norm': gain((n_mlstm, MLSTM_HEADS, MLSTM_HD)),
        'mlstm_skip': gain((n_mlstm, MLSTM_INNER)),
        'mlstm_w_down': normal((n_mlstm, MLSTM_INNER, d), MLSTM_INNER ** -0.5),
        'pool_w': normal((n_pool, len(POOL_WINDOWS), POOL_GROUP, POOL_GROUP), POOL_GROUP ** -0.5),
        'pool_b': normal((n_pool, len(POOL_WINDOWS), POOL_GROUP), 0.01),
        'pool_scale': gain((n_pool, d)),
        'final_g': gain((d,)),
    }

def second_block(x, c, ctx, c_ctx, ada_w, ada_b, norm1_g, norm2_g, mlp_w1, mlp_w2,
              gla_w_in, gla_w_a1, gla_w_a2, gla_b_a, gla_g_head, gla_w_o,
              mlstm_w_up, mlstm_conv_w, mlstm_conv_b, mlstm_w_qkv, mlstm_w_gate, mlstm_b_gate,
              mlstm_g_norm, mlstm_skip, mlstm_w_down,
              pool_w, pool_b, pool_scale, final_g):
    silu_c = jax.nn.silu(c)
    silu_cc = jax.nn.silu(c_ctx)
    h_lat, h_ctx = x, ctx
    for i in range(DEPTH_2):
        kind, j = i % N_MIXERS, i // N_MIXERS
        need_ctx = i < DEPTH_2 - 1
        mod_l = jnp.split((silu_c @ ada_w[i] + ada_b[i])[:, None, :], 6, axis=-1)
        mod_c = jnp.split((silu_cc @ ada_w[i] + ada_b[i])[None, None, :], 6, axis=-1)
        a_lat = modulate(rmsnorm(h_lat, norm1_g[i]), mod_l[0], mod_l[1])
        a_ctx = modulate(rmsnorm(h_ctx, norm1_g[i]), mod_c[0], mod_c[1])
        if kind == 0:
            o_ctx, o_lat = gla_mixer(a_ctx, a_lat, gla_w_in[j], gla_w_a1[j], gla_w_a2[j], gla_b_a[j],
                                     gla_g_head[j], gla_w_o[j], need_ctx)
        elif kind == 1:
            o_ctx, o_lat = mlstm_mixer(a_ctx, a_lat, mlstm_w_up[j], mlstm_conv_w[j], mlstm_conv_b[j],
                                       mlstm_w_qkv[j], mlstm_w_gate[j], mlstm_b_gate[j],
                                       mlstm_g_norm[j], mlstm_skip[j], mlstm_w_down[j], need_ctx)
        else:
            o_ctx, o_lat = pool_mixer(a_ctx, a_lat, pool_w[j], pool_b[j], pool_scale[j], need_ctx)
        h_lat = h_lat + mod_l[2] * o_lat
        h_lat = h_lat + mod_l[5] * sqrelu_mlp(modulate(rmsnorm(h_lat, norm2_g[i]), mod_l[3], mod_l[4]),
                                              mlp_w1[i], mlp_w2[i])
        if need_ctx:
            h_ctx = h_ctx + mod_c[2] * o_ctx
            h_ctx = h_ctx + mod_c[5] * sqrelu_mlp(modulate(rmsnorm(h_ctx, norm2_g[i]), mod_c[3], mod_c[4]),
                                                  mlp_w1[i], mlp_w2[i])
    return rmsnorm(h_lat, final_g)


def setup_inputs(seed=0):
    out = dict(first_inputs(seed))
    for name, value in second_inputs(seed + 1).items():
        if name != "x":
            out[name + "_2"] = value
    return out


def reference(
    x, a_mix_norm, a_w_in, a_conv, a_w_out, b_mix_norm, b_w_dq, b_q_norm, b_w_uq, b_w_o,
    kv_in_norm, w_dkv, kv_norm, w_ukv, ffn_norm, ffn_w_up, ffn_conv, ffn_w_down, final_norm,
    c_2, ctx_2, c_ctx_2, ada_w_2, ada_b_2, norm1_g_2, norm2_g_2, mlp_w1_2, mlp_w2_2, gla_w_in_2,
    gla_w_a1_2, gla_w_a2_2, gla_b_a_2, gla_g_head_2, gla_w_o_2, mlstm_w_up_2, mlstm_conv_w_2,
    mlstm_conv_b_2, mlstm_w_qkv_2, mlstm_w_gate_2, mlstm_b_gate_2, mlstm_g_norm_2, mlstm_skip_2,
    mlstm_w_down_2, pool_w_2, pool_b_2, pool_scale_2, final_g_2,
):
    x = first_block(
        x, a_mix_norm, a_w_in, a_conv, a_w_out, b_mix_norm, b_w_dq, b_q_norm, b_w_uq, b_w_o,
        kv_in_norm, w_dkv, kv_norm, w_ukv, ffn_norm, ffn_w_up, ffn_conv, ffn_w_down, final_norm,
    )
    return second_block(
        x, c_2, ctx_2, c_ctx_2, ada_w_2, ada_b_2, norm1_g_2, norm2_g_2, mlp_w1_2, mlp_w2_2,
        gla_w_in_2, gla_w_a1_2, gla_w_a2_2, gla_b_a_2, gla_g_head_2, gla_w_o_2, mlstm_w_up_2,
        mlstm_conv_w_2, mlstm_conv_b_2, mlstm_w_qkv_2, mlstm_w_gate_2, mlstm_b_gate_2,
        mlstm_g_norm_2, mlstm_skip_2, mlstm_w_down_2, pool_w_2, pool_b_2, pool_scale_2,
        final_g_2,
    )


_drawn_inputs = setup_inputs


def setup_inputs(seed=0):
    import zlib

    import numpy as np

    out = dict(_drawn_inputs(seed))
    spreads = {}
    factors = {'b_mix_norm': 8.0,
     'b_q_norm': 8.0,
     'kv_in_norm': 8.0,
     'kv_norm': 8.0,
     'ffn_norm': 3.268,
     'final_norm': 2.715,
     'ada_b_2': 3.254,
     'norm1_g_2': 6.989,
     'norm2_g_2': 19.681,
     'gla_b_a_2': 6.241,
     'gla_g_head_2': 8.0,
     'final_g_2': 7.732}
    for name, (base, spread) in spreads.items():
        noise = np.random.default_rng([zlib.crc32(name.encode()), seed]).standard_normal(out[name].shape)
        drawn = base * np.exp(spread * noise) if base else spread * noise
        out[name] = jnp.asarray(drawn.astype(out[name].dtype))
    for name, factor in factors.items():
        out[name] = (out[name] * factor).astype(out[name].dtype)
    return out
```

```python
from contextlib import ExitStack, contextmanager

import numpy as np

import concourse.bass as bass
from concourse import mybir

F32 = mybir.dt.float32
F32R = mybir.dt.float32r
ALU = mybir.AluOpType
ACT = mybir.ActivationFunctionType
AX = mybir.AxisListType

P = 128
T = 256
D = 1024
DC = D // P
FF = 2816
FC = FF // P
HEADS = 8
HP = HEADS // 2
RQ = 512 // P
RK = 256 // P
GH = 4
CH = 64
MC = 4096 // P
EPS = 1e-6
QK_SCALE = (128 + 64) ** -0.5
GLA_SCALE = 128 ** -0.5
INV_TAU = 1.0 / 16.0
RING = 4
LEAD = 3
BLK = 8

PHASES = [("mix_in", 3 * DC), ("mix_out", DC), ("up0", 2 * FC), ("down0", 3 * DC), ("dkv", 4), ("dq", 4),
          ("ukv", 4), ("uq", 8), ("attn_out", DC), ("up1", 2 * FC), ("down1", 3 * DC),
          ("gla_q", 4), ("gla_k", 4), ("gla_v", 8), ("gla_r", 8), ("ctx_k", 4), ("ctx_v", 8),
          ("gla_out", DC), ("mlp_up", MC), ("mlp_down", MC)]
UNITS = sum(n for _, n in PHASES)

VEC = {}
for _name, _n in [("g_mix0", 8), ("g_ffn0", 8), ("g_kvin", 8), ("g_mix1", 8), ("g_q", 4), ("g_kv", 2),
                  ("g_ffn1", 8), ("g_fin1", 8), ("g_n1", 8), ("g_n2", 8), ("g_fin2", 8), ("g_head", 8),
                  ("b_gate", 8), ("b_ada", 48), ("c", 8), ("c_ctx", 8), ("conv_mix", 3 * DC),
                  ("conv0", 3 * 2 * FC), ("conv1", 3 * 2 * FC)]:
    VEC[_name] = sum(n for _, n in VEC.values()), _n
NVEC = sum(n for _, n in VEC.values())

CST = {}
for _name, _n in [("ones", P), ("ident", P), ("mask_f", 3 * P), ("mask_b", 3 * P)]:
    CST[_name] = sum(n for _, n in CST.values()), _n
NCST = sum(n for _, n in CST.values())
ROT = {}
for _name, _n in [("mask_s", 3 * P), ("cos_q", T), ("sin_q", T), ("cos_a", T), ("sin_a", T), ("cos_b", T), ("sin_b", T)]:
    ROT[_name] = sum(n for _, n in ROT.values()), _n
NROT = sum(n for _, n in ROT.values())


class Counts:

    def __init__(self, eng):
        self.eng, self.n, self.i, self.per, self.start = eng, {}, None, {}, {}

    def value(self, sem, extra=0):
        n = self.n.get(sem.name, 0) + extra
        if self.i is None or not self.per.get(sem.name):
            return n
        return self.i * self.per[sem.name] + n

    def take(self, sem, by=1):
        self.n[sem.name] = self.n.get(sem.name, 0) + by
        self.eng.wait_ge(sem, self.value(sem))

    def sig(self, ins, sem, by=1):
        self.n[sem.name] = self.n.get(sem.name, 0) + by
        ins.then_inc(sem, by)

    def again(self, sem, back=0):
        if self.n.get(sem.name, 0) - back > 0:
            self.eng.wait_ge(sem, self.value(sem, -back))

    @contextmanager
    def loop(self, times, per):
        with self.eng.Fori(0, times) as i:
            self.i, self.per, self.start = i, {s.name: k for s, k in per.items()}, dict(self.n)
            yield i
        for name in {*self.n, *self.per}:
            k = self.n.get(name, 0) - self.start.get(name, 0)
            assert k == self.per.get(name, 0), (name, k, self.per.get(name, 0))
            self.n[name] = self.start.get(name, 0) + k * times
        self.i, self.per = None, {}


def at(t, k):
    return t[:, k * T:(k + 1) * T] if isinstance(k, int) else t[:, bass.ds(k * T, T)]


def program(nc, stream, xT, ctxT, vec, cst, rot, wa1, wa2, ada, out):
    ctx = ExitStack()

    def sb(name, cols, dt=F32, stack=ctx, rows=P):
        return stack.enter_context(nc.sbuf_tensor(name, [rows, cols], dt))

    with ctx:
        raw = sb("raw", RING * D)
        whi = sb("whi", RING * D, F32R)
        wlo = sb("wlo", RING * D, F32R)
        h = sb("h", DC * T)
        vt = sb("vt", NVEC)
        ct = sb("ct", NCST)
        wa1s = sb("wa1s", DC * 32)
        wa2s = sb("wa2s", D, rows=32)
        rstd = sb("rstd", T)
        root = sb("root", T)
        ssum = sb("ssum", T)
        sq = sb("sq", 2 * T)
        mod = sb("mod", 64)
        gmod = sb("gmod", 3 * DC)
        sc = sb("sc", 16)
        state = sb("state", 2 * GH * T)
        stage = ExitStack()
        xhi = sb("xhi", DC * T, F32R, stage)
        xlo = sb("xlo", DC * T, F32R, stage)
        stage.close()
        stage = ExitStack()
        ck = sb("ck", GH * T, F32, stage)
        cval = sb("cval", 2 * D, F32, stage)
        kt = sb("kt", 2 * GH * P, F32, stage)
        stage.close()
        sb("x_held", 2 * DC * T)
        stage = ExitStack()
        yhi = sb("yhi", FC * T, F32R, stage)
        ylo = sb("ylo", FC * T, F32R, stage)
        U = sb("U", 4 * (T + 2), F32, stage)
        cv = sb("cv", 4 * T, F32, stage)
        sil = sb("sil", 2 * T, F32, stage)
        prod = sb("prod", 2 * T, F32, stage)
        stage.close()
        EARLY = 2 * HEADS * T + HEADS * T + HP * T + HEADS * T + 2 * T + 2 * D + 4 * RQ * T + 4 * RK * T + 6 * T + 4 * 3 * P + 16
        stage = ExitStack()
        ohi = sb("ohi", HEADS * T, F32R, stage)
        olo = sb("olo", HEADS * T, F32R, stage)
        qn = sb("qn", HEADS * T, F32, stage)
        qr = sb("qr", HP * T, F32, stage)
        kn = sb("kn", HEADS * T, F32, stage)
        kr = sb("kr", 2 * T, F32, stage)
        vv = sb("vv", 2 * D, F32, stage)
        cf = sb("cf", RQ * T, F32, stage)
        chi = sb("chi", RQ * T, F32R, stage)
        clo = sb("clo", RQ * T, F32R, stage)
        csq = sb("csq", RQ * T, F32, stage)
        kf = sb("kf", RK * T, F32, stage)
        khi = sb("khi", RK * T, F32R, stage)
        klo = sb("klo", RK * T, F32R, stage)
        ksq = sb("ksq", RK * T, F32, stage)
        rk = sb("rk", T, F32, stage)
        rq = sb("rq", T, F32, stage)
        rt = sb("rt", 4 * T, F32, stage)
        sm = sb("sm", 2 * 3 * P, F32, stage)
        mx = sb("mx", 2 * 8, F32, stage)
        pt = sb("pt", 2 * 3 * P, F32, stage)
        stage.close()
        stage = ExitStack()
        sb("stacks_held", EARLY, F32, stage)
        rt_tab = sb("rt_tab", NROT, F32, stage)
        ada_w = sb("ada_w", 2 * D, F32, stage)
        ada_p = sb("ada_p", D, F32, stage)
        ada_acc = sb("ada_acc", 2 * D, F32, stage)
        stage.close()
        stage = ExitStack()
        zhi = sb("zhi", DC * T, F32R, stage)
        zlo = sb("zlo", DC * T, F32R, stage)
        a32 = sb("a32", DC * T, F32, stage)
        gq = sb("gq", GH * T, F32, stage)
        gk = sb("gk", GH * T, F32, stage)
        gv = sb("gv", 2 * D, F32, stage)
        rsil = sb("rsil", DC * T, F32, stage)
        t1 = sb("t1", T, F32, stage, rows=32)
        za = sb("za", GH * T, F32, stage)
        zm = sb("zm", GH * T, F32, stage)
        pb = sb("pb", GH * (T + 1), F32, stage)
        one_t = sb("one_t", T, F32, stage)
        qd = [sb(f"qd{d}", GH * T, F32, stage) for d in range(2)]
        ki = [sb(f"ki{d}", GH * T, F32, stage) for d in range(2)]
        kw = [sb(f"kw{d}", GH * 2 * CH, F32, stage) for d in range(2)]
        qk = [sb(f"qk{d}", GH * T, F32, stage) for d in range(2)]
        qf = [sb(f"qf{d}", GH * T, F32, stage) for d in range(2)]
        att = sb("att", 4 * 3 * P, F32, stage)
        osq = sb("osq", 2 * T, F32, stage)
        stage.close()
        stage = ExitStack()
        mhi = sb("mhi", MC * T, F32R, stage)
        mlo = sb("mlo", MC * T, F32R, stage)
        mr = sb("mr", 4 * T, F32, stage)
        ms = sb("ms", 4 * T, F32, stage)
        stage.close()
        ps = [ctx.enter_context(nc.psum_tensor(f"ps{i}", [P, 512], F32)) for i in range(8)]
        STAT = ps[4]

        named = {}

        def ev(name):
            if name not in named:
                named[name] = ctx.enter_context(nc.semaphore(name))
            return named[name]

        raw_ready = [ev(f"raw_ready{i}") for i in range(RING)]
        hi_ready = ev("hi_ready")
        lo_ready = ev("lo_ready")
        pe_units = ev("pe_units")
        tile_read = ev("tile_read")
        xhi_ready = ev("xhi_ready")
        x_ready = ev("x_ready")
        sq_ready = ev("sq_ready")
        ssum_ready = ev("ssum_ready")
        stat_ready = ev("stat_ready")
        root_ready = ev("root_ready")
        rstd_ready = ev("rstd_ready")
        u_ready = ev("u_ready")
        tap_ready = ev("tap_ready")
        conv_ready = ev("conv_ready")
        sil_ready = ev("sil_ready")
        y_f32 = ev("y_f32")
        yhi_ready = ev("yhi_ready")
        y_ready = ev("y_ready")
        a_ready = ev("a_ready")
        seq_dve = ev("seq_dve")

        def col(name, k=0):
            return vt[:, VEC[name][0] + k:VEC[name][0] + k + 1]

        def cst_of(name):
            return ct[:, CST[name][0]:CST[name][0] + CST[name][1]]

        def rot_of(name):
            return rt_tab[:, ROT[name][0]:ROT[name][0] + ROT[name][1]]

        ones, ident = cst_of("ones"), cst_of("ident")
        block = ctx.enter_context(nc.Block())

        @block.sync
        def _(sp):
            def load_group(first, done):
                for j in range(RING):
                    if done is not None:
                        sp.wait_ge(lo_ready, done + (j + 1))
                    sp.dma_start(raw[:, j * D:(j + 1) * D], stream[first + j]).then_inc(raw_ready[j], 16)

            sp.dma_start(h[:, :], xT).then_inc(ev("x_loaded"), 16)
            sp.dma_start(vt[:, :], vec).then_inc(ev("tables"), 16)
            sp.dma_start(ct[:, :], cst).then_inc(ev("tables"), 16)
            load_group(0, None)
            sp.dma_start(wa1s[:, :], wa1).then_inc(ev("tables_late"), 16)
            sp.dma_start(wa2s[:, :], wa2).then_inc(ev("tables_late"), 16)
            sp.dma_start(rt_tab[:, :], rot).then_inc(ev("tables_late"), 16)
            with sp.Fori(0, UNITS // RING - 1) as g:
                load_group(g * RING + RING, g * RING)
            for k in range(DC):
                sp.wait_ge(ev("out_chunk"), k + 1)
                sp.dma_start(out[:, k * T:(k + 1) * T], at(h, k)).then_inc(ev("stored"), 16)
            sp.wait_ge(ev("stored"), 16 * DC)

        @block.gpsimd
        def _(pool):
            c = Counts(pool)
            added = ev("ada_added")

            def weighted(b, scalar, acc):
                dst = ada_acc[:, acc * D:(acc + 1) * D]
                pool.wait_ge(ev("sc_ready"), 1)
                c.sig(pool.tensor_tensor(ada_p[:, :], ada_w[:, b * D:(b + 1) * D], scalar.to_broadcast([P, D]),
                                         ALU.mult), added)
                c.again(added)
                c.sig(pool.tensor_tensor(dst, dst, ada_p[:, :], ALU.add), added)
                c.again(added)

            pool.wait_ge(ev("sc_ready"), 1)
            for s in range(6):
                accs = (0, 1) if s < 2 else (s % 2,)
                if s in (1, 2, 4):
                    pool.wait_ge(ev("ada_summed"), {1: 2, 2: 4, 4: 6}[s])
                for acc in accs:
                    c.sig(pool.memset(ada_acc[:, acc * D:(acc + 1) * D], 0.0), added)
                c.again(added)
                for b in range(2):
                    pool.dma_start(ada_w[:, b * D:(b + 1) * D], ada[s * DC + b]).then_inc(ev(f"ada_ready{b}"), 16)

                def two_rows(k, last):
                    for b in range(2):
                        c.take(ev(f"ada_ready{b}"), 16)
                        for acc in accs:
                            j = k + (b + (DC if s < 2 and acc else 0))
                            weighted(b, sc[:, j:j + 1] if isinstance(j, int) else sc[:, bass.ds(j, 1)], acc)
                        if not last:
                            pool.wait_ge(ev("sc_ready"), 1)
                            pool.dma_start(ada_w[:, b * D:(b + 1) * D], ada[k + (s * DC + b + 2)])\
                                .then_inc(ev(f"ada_ready{b}"), 16)

                with c.loop(DC // 2 - 1, {added: 4 * len(accs), ev("ada_ready0"): 16, ev("ada_ready1"): 16}) as i:
                    two_rows(i * 2, False)
                two_rows(DC - 2, True)
                pool.engine_nop().then_inc(ev("ada_piece"), 1)

        @block.tensor
        def _(pe):
            c = Counts(pe)
            tile = [0]
            tiles_per = [0]

            def tile_free(n, lag):
                if c.i is not None:
                    pe.wait_ge(tile_read, c.i * tiles_per[0] + (n - lag + 1))
                elif n - lag + 1 > 0:
                    pe.wait_ge(tile_read, n - lag + 1)

            def slot_of_next_unit():
                c.take(lo_ready)
                return (c.n["lo_ready"] - 1) % RING

            def units(n, K, hi, lo, sizes=(BLK,), lag=RING):
                blk = 0
                for j in range(n):
                    slot = slot_of_next_unit()
                    for b in range(sizes[j % len(sizes)]):
                        t, k = tile[0] + blk // K, blk % K
                        if k == 0:
                            tile_free(t, lag)
                        dst = ps[t % lag][:, 0:T]
                        w = slice(slot * D + b * P, slot * D + (b + 1) * P)
                        pe.matmul(dst, whi[:, w], at(hi, k), start=(k == 0), stop=False)
                        pe.matmul(dst, whi[:, w], at(lo, k), start=False, stop=False)
                        last = pe.matmul(dst, wlo[:, w], at(hi, k), start=False, stop=(k == K - 1))
                        blk += 1
                    c.sig(last, pe_units)
                tile[0] += blk // K

            def looped(times, n, K, hi, lo, sizes=(BLK,), lag=RING):
                t = tile[0]
                tiles_per[0] = sum(sizes[j % len(sizes)] for j in range(n)) // K
                with c.loop(times, {lo_ready: n, pe_units: n}):
                    units(n, K, hi, lo, sizes, lag)
                tile[0] = t + times * tiles_per[0]

            def moving(parts, hi, lo):
                for unit in parts:
                    slot = slot_of_next_unit()
                    for half, (k, pair, first, final) in enumerate(unit):
                        w = slice(slot * D + half * 512, slot * D + (half + 1) * 512)
                        for tk in range(2):
                            t = tile[0] + 2 * pair + tk
                            dst = ps[t % RING][:, :]
                            tok = slice(k * T + tk * P, k * T + (tk + 1) * P)
                            if first:
                                tile_free(t, RING)
                            pe.matmul(dst, hi[:, tok], whi[:, w], start=first, stop=False)
                            pe.matmul(dst, lo[:, tok], whi[:, w], start=False, stop=False)
                            last = pe.matmul(dst, hi[:, tok], wlo[:, w], start=False, stop=final)
                    c.sig(last, pe_units)
                tile[0] += 4

            V_PARTS = [[(2 * j % DC + b, j // 4, 2 * j % DC + b == 0, 2 * j % DC + b == DC - 1) for b in range(2)]
                       for j in range(8)]

            def stat_of(pieces):
                c.n["root_ready"] = c.n.get("stat_ready", 0)
                c.again(root_ready)
                for k, piece in enumerate(pieces):
                    last = pe.matmul(STAT[:, 0:T], ones, piece, start=(k == 0), stop=(k == len(pieces) - 1))
                c.sig(last, stat_ready)

            def stat():
                c.take(ssum_ready, 8)
                stat_of([ssum[:, :]])

            def ada_sums(s, acc, at_col):
                pe.wait_ge(ev("ada_piece"), s + 1)
                for m in range(DC):
                    last = pe.matmul(ps[7][:, at_col * DC + m:at_col * DC + m + 1],
                                     ada_acc[:, acc * D + m * P:acc * D + (m + 1) * P], ones[:, 0:1],
                                     start=True, stop=True)
                last.then_inc(ev("ada_summed"), 1)

            pe.wait_ge(ev("tables"), 32)
            c.take(x_ready, 8)
            stat()
            units(3 * DC, DC, xhi, xlo)
            c.take(y_ready, 8)
            units(DC, DC, yhi, ylo)
            c.take(x_ready, 8)
            stat()
            looped(FC // 2, 4, DC, xhi, xlo)
            ada_sums(0, 0, 0)
            ada_sums(0, 1, 6)
            c.take(y_ready, FC)
            looped(2, 12, FC, yhi, ylo, (8, 8, 6))
            c.take(x_ready, 8)
            stat()
            units(4, DC, xhi, xlo)
            c.take(x_ready, 8)
            units(4, DC, ohi, olo)
            ada_sums(1, 0, 1)
            ada_sums(1, 1, 7)
            pe.wait_ge(ev("kv_squares"), 1)
            stat_of([at(ksq, k) for k in range(RK)])
            pe.wait_ge(ev("q_squares"), 1)
            stat_of([at(csq, k) for k in range(RQ)])
            pe.wait_ge(ev("kv_latent"), 1)
            units(2, RK, khi, klo)
            moving([[(k, n, k == 0, k == RK - 1) for n in range(2)] for k in range(RK)], khi, klo)
            pe.wait_ge(ev("q_latent"), 1)
            units(8, RQ, chi, clo)
            pe.wait_ge(ev("queries"), HP)

            def scores(hd):
                if hd >= 2:
                    pe.wait_ge(ev("masked"), hd - 1)
                for q in range(2):
                    o = ps[hd % 2][:, q * P:q * P + (q + 1) * P]
                    keys = (q + 1) * P
                    pe.matmul(o, qn[:, hd * T + q * P:hd * T + (q + 1) * P], kn[:, hd * T:hd * T + keys],
                              start=True, stop=False)
                    last = pe.matmul(o, qr[:, hd // 2 * T + q * P:hd // 2 * T + (q + 1) * P],
                                     kr[:, hd % 2 * T:hd % 2 * T + keys], start=False, stop=True)
                last.then_inc(ev("scores"), 1)

            def turn(hd):
                pe.wait_ge(ev("weights"), hd + 1)
                if hd >= 2:
                    pe.wait_ge(ev("turned_read"), hd - 1)
                for s in range(3):
                    o = hd % 2 * 3 * P + s * P
                    last = pe.transpose(ps[2 + hd % 2][:, s * P:(s + 1) * P], sm[:, o:o + P], ident)
                last.then_inc(ev("turned"), 1)

            x_before = c.n["x_ready"]

            def values(hd):
                pe.wait_ge(ev("turned_read"), hd + 1)
                if hd >= 2:
                    pe.wait_ge(x_ready, x_before + hd - 1)
                o, p0 = ps[5 + hd % 2], hd % 2 * 3 * P
                pe.matmul(o[:, 0:T], vv[:, hd * P:(hd + 1) * P], pt[:, p0:p0 + T], start=True, stop=False)
                pe.matmul(o[:, P:T], vv[:, D + hd * P:D + (hd + 1) * P], pt[:, p0 + T:p0 + 3 * P], start=False, stop=True)\
                    .then_inc(ev("head_out"), 1)

            scores(0)
            scores(1)
            for hd in range(HEADS + 1):
                if hd < HEADS:
                    turn(hd)
                    if hd + 2 < HEADS:
                        scores(hd + 2)
                if hd >= 1:
                    values(hd - 1)
            c.take(x_ready, 8)
            ada_sums(2, 0, 2)
            ada_sums(3, 1, 3)
            units(DC, DC, ohi, olo)
            c.take(x_ready, 8)
            stat()
            looped(FC // 2, 4, DC, xhi, xlo)
            ada_sums(4, 0, 4)
            ada_sums(5, 1, 5)
            c.take(y_ready, FC)
            looped(2, 12, FC, yhi, ylo, (8, 8, 6))

            def gate_in(n):
                for k in range(DC):
                    last = pe.matmul(ps[7][0:32, 0:T], wa1s[:, k * 32:(k + 1) * 32], at(a32, k),
                                     start=(k == 0), stop=(k == DC - 1))
                last.then_inc(ev("gate_in"), 1)

            def gate_out(n, d):
                i = 2 * n + d
                pe.wait_ge(ev("gate_in_read"), n + 1)
                if i:
                    pe.wait_ge(ev("gate_read"), i)
                for m in range(GH):
                    last = pe.matmul(ps[5 + m // 2][:, m % 2 * T:(m % 2 + 1) * T],
                                     wa2s[:, (d * GH + m) * P:(d * GH + m + 1) * P], t1[:, :], start=True, stop=True)
                last.then_inc(ev("gate_out"), 1)

            stat()
            stat()
            c.take(x_ready, 8)
            pe.wait_ge(ev("tables_late"), 48)
            units(8, DC, xhi, xlo)
            gate_in(0)
            gate_out(0, 0)
            moving(V_PARTS, xhi, xlo)
            stat()
            units(8, DC, xhi, xlo)
            c.take(x_ready, 8)
            units(4, DC, zhi, zlo)
            gate_out(0, 1)
            gate_in(1)
            moving(V_PARTS, zhi, zlo)
            for d in range(2):
                gate_out(1, d)
            pe.wait_ge(tile_read, tile[0])
            for d in range(2):
                pe.wait_ge(ev("ctx_decayed"), d + 1)
                for tk in range(2):
                    if 2 * d + tk:
                        pe.wait_ge(ev("ctx_turned_read"), 2 * d + tk)
                    for m in range(GH):
                        o = (d * GH + m) * T + tk * P
                        last = pe.transpose(ps[7][:, m * P:(m + 1) * P], a32[:, o:o + P], ident)
                    last.then_inc(ev("ctx_turned"), 1)
                pe.wait_ge(ev("ctx_turned_read"), 2 * d + 2)
                for m in range(GH):
                    dst = ps[2 * d + m // 2][:, m % 2 * T:(m % 2 + 1) * T]
                    for tk in range(2):
                        last = pe.matmul(dst, kt[:, (tk * GH + m) * P:(tk * GH + m + 1) * P],
                                         cval[:, tk * D + m * T:tk * D + (m + 1) * T], start=(tk == 0), stop=(tk == 1))
                last.then_inc(ev("state_out"), 1)

            pe.wait_ge(ev("state_read"), 2)
            pe.wait_ge(ev("decayed"), 2)

            def gla_scores(n):
                hd, d = n // 2, n % 2
                dst = ps[n % 4]
                if n >= 4:
                    pe.wait_ge(ev("gla_masked"), n - 3)
                o = hd * T
                for b in range(2):
                    c0 = 2 * P * b
                    pe.matmul(dst[:, c0:c0 + P], ki[d][:, o + b * P:o + (b + 1) * P],
                              qd[d][:, o + b * P:o + (b + 1) * P], start=True, stop=True)
                    keys = kw[d][:, (hd * 2 + b) * CH:(hd * 2 + b + 1) * CH]
                    if d == 0:
                        pe.matmul(dst[0:CH, c0 + CH:c0 + P], keys, qd[d][:, o + b * P + CH:o + (b + 1) * P],
                                  start=True, stop=True)
                    else:
                        pe.matmul(dst[CH:P, c0:c0 + CH], keys, qd[d][:, o + b * P:o + b * P + CH],
                                  start=True, stop=True)
                k0, q0 = (o, o + P) if d == 0 else (o + P, o)
                pe.matmul(dst[:, P:2 * P], qk[d][:, k0:k0 + P], qk[d][:, q0:q0 + P], start=True, stop=True)\
                    .then_inc(ev("gla_scores"), 1)

            def gla_values(hd):
                pe.wait_ge(ev("gla_masked"), 2 * hd + 2)
                if hd >= 2:
                    pe.wait_ge(ev("gla_read"), hd - 1)
                a0, a1 = (2 * hd) % 4 * 3 * P, (2 * hd + 1) % 4 * 3 * P
                for vc in range(2):
                    o = ps[5 + hd % 2][:, vc * T:(vc + 1) * T]
                    v = hd * T + vc * P
                    pe.matmul(o, state[:, v:v + P], at(qf[0], hd), start=True, stop=False)
                    pe.matmul(o, state[:, GH * T + v:GH * T + v + P], at(qf[1], hd), start=False, stop=False)
                    pe.matmul(o, gv[:, v:v + P], att[:, a0:a0 + T], start=False, stop=False)
                    pe.matmul(o, gv[:, D + v:D + v + P], att[:, a1 + P:a1 + 3 * P], start=False, stop=False)
                    pe.matmul(o[:, P:T], gv[:, D + v:D + v + P], att[:, a0 + T:a0 + 3 * P], start=False, stop=False)
                    last = pe.matmul(o[:, 0:P], gv[:, v:v + P], att[:, a1:a1 + P], start=False, stop=True)
                last.then_inc(ev("gla_out"), 1)

            for n in range(4):
                gla_scores(n)
            for hd in range(GH + 1):
                if hd < GH:
                    gla_values(hd)
                if hd + 2 < GH:
                    gla_scores(2 * hd + 4)
                    gla_scores(2 * hd + 5)
                if hd >= 1:
                    pe.wait_ge(ev("gla_squares"), hd)
                    stat_of([osq[:, 0:T], osq[:, T:2 * T]])
            c.take(y_ready, 8)
            units(DC, DC, zhi, zlo)
            stat()
            c.take(x_ready, 8)
            looped(MC // 4, 4, DC, xhi, xlo)
            c.take(y_ready, MC)
            looped(DC // 2, 8, MC, mhi, mlo, lag=2)
            stat()

        @block.scalar
        def _(act):
            c = Counts(act)

            def settled():
                act.wait_ge(ev("tables"), 32)

            def hi(n=1):
                for _ in range(n):
                    u = c.n.get("hi_ready", 0)
                    if u >= UNITS:
                        return
                    s = u % RING
                    landed = 16 * (u // RING + 1)
                    if c.i is not None:
                        landed = c.i * (4 * c.per["hi_ready"]) + landed
                    act.wait_ge(raw_ready[s], landed)
                    if u >= RING:
                        act.wait_ge(pe_units, c.value(hi_ready, 1 - RING))
                    c.sig(act.activation(whi[:, s * D:(s + 1) * D], raw[:, s * D:(s + 1) * D], ACT.Copy), hi_ready)

            def square(src, k, slot):
                if c.n.get("sq_ready", 0) >= 2:
                    added = c.value(sq_ready, -1)
                    if c.i is not None:
                        added = act.to_reg(added)
                        settled()
                    act.wait_ge(ssum_ready, added)
                c.sig(act.activation(at(sq, slot % 2), at(src, k), ACT.Square), sq_ready)

            def sqrt_stat(n):
                c.n["rstd_ready"] = c.n.get("root_ready", 0)
                c.again(rstd_ready)
                c.take(stat_ready)
                c.sig(act.activation(root[:, :], STAT[:, 0:T], ACT.Sqrt, scale=1.0 / n, bias=EPS), root_ready)

            def ffn_up(conv):
                base = VEC[conv][0]
                with c.loop(FC // 2, {hi_ready: 4, tile_read: 4, tap_ready: 4, conv_ready: 4, sil_ready: 2,
                                      y_f32: 2, yhi_ready: 2}) as i:
                    def tap(j):
                        settled()
                        c.take(tile_read)
                        c.sig(act.activation(at(cv, j), U[:, j * (T + 2) + 2:(j + 1) * (T + 2)], ACT.Copy,
                                             scale=vt[:, bass.ds(i * 12 + (base + 3 * j + 2), 1)]), tap_ready)

                    def silu(f):
                        c.take(conv_ready)
                        c.sig(act.activation(at(sil, f), at(cv, 2 * f), ACT.Silu), sil_ready)
                        c.n["conv_ready"] += 1

                    def yh(f):
                        settled()
                        c.take(y_f32)
                        c.sig(act.activation(at(yhi, i * 2 + f), at(prod, f), ACT.Copy), yhi_ready)

                    hi()
                    tap(0)
                    hi()
                    tap(1)
                    silu(0)
                    hi()
                    tap(2)
                    yh(0)
                    hi()
                    tap(3)
                    silu(1)
                    yh(1)

            def resid(units_per, gain):
                per = {hi_ready: 4 * units_per, tile_read: 4, sq_ready: 4}
                if gain:
                    per[xhi_ready] = 4
                with c.loop(2, per) as i:
                    for m in range(4):
                        hi(units_per)
                        settled()
                        c.take(tile_read)
                        if gain:
                            c.sig(act.activation(at(xhi, i * 4 + m), at(h, i * 4 + m), ACT.Copy,
                                                 scale=vt[:, bass.ds(i * 4 + (VEC[gain][0] + m), 1)]), xhi_ready)
                        square(h, i * 4 + m, m)

            act.wait_ge(ev("tables"), 32)
            act.activation(sc[:, :], vt[:, VEC["c"][0]:VEC["c"][0] + 16], ACT.Silu).then_inc(ev("sc_ready"), 1)
            act.wait_ge(ev("x_loaded"), 16)
            for k in range(DC):
                c.sig(act.activation(at(xhi, k), at(h, k), ACT.Copy, scale=col("g_mix0", k)), xhi_ready)
                square(h, k, k)
            hi(LEAD)
            sqrt_stat(D)
            with c.loop(2, {hi_ready: 12, u_ready: 4, tap_ready: 4, y_f32: 4, yhi_ready: 4}) as i:
                for j in range(4):
                    hi(2)
                    settled()
                    c.take(u_ready)
                    c.sig(act.activation(at(cv, j), U[:, j * (T + 2) + 2:(j + 1) * (T + 2)], ACT.Copy,
                                         scale=vt[:, bass.ds(i * 12 + (VEC["conv_mix"][0] + 3 * j + 2), 1)]), tap_ready)
                    hi()
                    settled()
                    c.take(y_f32)
                    c.sig(act.activation(at(yhi, i * 4 + j), at(prod, j % 2), ACT.Copy), yhi_ready)
            c.n["tile_read"] = 3 * DC
            resid(1, "g_ffn0")
            sqrt_stat(D)
            ffn_up("conv0")
            resid(3, "g_kvin")
            sqrt_stat(D)
            for u in range(4):
                hi()
                for k in range(2 * u, 2 * u + 2):
                    c.sig(act.activation(at(ohi, k), at(h, k), ACT.Copy, scale=col("g_mix1", k)), xhi_ready)
            c.take(tile_read, 2)
            act.activation(ksq[:, :], kf[:, :], ACT.Square).then_inc(ev("kv_squares"), 1)
            hi(4)
            c.take(tile_read, 6)
            act.activation(csq[:, :], cf[:, :], ACT.Square).then_inc(ev("q_squares"), 1)
            sqrt_stat(RK * P)
            sqrt_stat(RQ * P)
            act.wait_ge(ev("kv_normed"), 1)
            act.activation(khi[:, :], kf[:, :], ACT.Copy).then_inc(ev("khi_ready"), 1)
            act.wait_ge(ev("q_normed"), 1)
            act.activation(chi[:, :], cf[:, :], ACT.Copy).then_inc(ev("chi_ready"), 1)
            hi(12)
            c.n["tile_read"] += 8 + 4 + 16
            for hd in range(HEADS + 2):
                if hd < HEADS:
                    act.wait_ge(ev("negmax"), hd + 1)
                    m0 = hd % 2 * 8
                    for q in range(2):
                        s0 = hd % 2 * 3 * P + q * P
                        s = sm[:, s0:s0 + (q + 1) * P]
                        last = act.activation(s, s, ACT.Exp, bias=mx[:, m0 + 2 + q:m0 + 3 + q],
                                              accum_out=mx[:, m0 + 4 + q:m0 + 5 + q])
                    last.then_inc(ev("exps"), 1)
                if 1 <= hd <= HEADS:
                    g = hd - 1
                    act.wait_ge(ev("turned"), g + 1)
                    if g >= 2:
                        act.wait_ge(ev("head_out"), g - 1)
                    act.activation(pt[:, g % 2 * 3 * P:(g % 2 + 1) * 3 * P], ps[2 + g % 2][:, 0:3 * P], ACT.Copy)\
                        .then_inc(ev("turned_read"), 1)
                if hd >= 2:
                    g = hd - 2
                    act.wait_ge(ev("head_out"), g + 1)
                    c.sig(act.activation(at(ohi, g), ps[5 + g % 2][:, 0:T], ACT.Copy), xhi_ready)
            resid(1, "g_ffn1")
            sqrt_stat(D)
            ffn_up("conv1")
            resid(3, None)

            def modulated(dst):
                for k in range(DC):
                    c.take(a_ready)
                    c.sig(act.activation(at(dst, k), at(a32, k), ACT.Copy), xhi_ready)

            def log_gate(i):
                act.wait_ge(ev("gate_out"), i + 1)
                for m in range(GH):
                    last = act.activation(at(za, m), ps[5 + m // 2][:, m % 2 * T:(m % 2 + 1) * T], ACT.Abs,
                                          bias=col("b_gate", i % 2 * GH + m))
                last.then_inc(ev("gate_abs"), 1)
                act.wait_ge(ev("gate_abs"), i + 1)
                act.activation(za[:, :], za[:, :], ACT.Exp, scale=-1.0).then_inc(ev("gate_exp"), 1)
                act.wait_ge(ev("gate_exp"), i + 1)
                act.activation(za[:, :], za[:, :], ACT.Ln, bias=1.0).then_inc(ev("gate_ln"), 1)

            def by_head(t, w=T):
                return t[:, :].rearrange("p (m t) -> p m t", t=w)

            def decays(d):
                s = INV_TAU if d == 0 else -INV_TAU
                n = 4 * d
                act.wait_ge(ev("expo"), n + 1)
                act.activation(qd[d][:, :], za[:, :], ACT.Exp, scale=s)
                act.activation(ki[d][:, :], za[:, :], ACT.Exp, scale=-s).then_inc(ev("factors"), 1)
                act.wait_ge(ev("expo"), n + 2)
                act.activation(by_head(qk[d])[:, :, 0:P], by_head(zm)[:, :, 0:P], ACT.Exp, scale=-INV_TAU)
                act.activation(by_head(qk[d])[:, :, P:T], by_head(zm)[:, :, P:T], ACT.Exp, scale=INV_TAU)\
                    .then_inc(ev("factors"), 1)
                act.wait_ge(ev("expo"), n + 3)
                act.activation(kw[d][:, :], za[:, 0:GH * 2 * CH], ACT.Exp, scale=-s).then_inc(ev("factors"), 1)
                act.wait_ge(ev("expo"), n + 4)
                act.activation(qf[d][:, :], zm[:, :], ACT.Exp, scale=s).then_inc(ev("factors"), 1)

            sqrt_stat(D)
            for k in range(DC):
                act.wait_ge(ev("fin_ready"), k + 1)
                square(h, k, k)
            sqrt_stat(D)
            modulated(xhi)
            hi(8)
            c.take(tile_read, 8)
            act.wait_ge(ev("gate_in"), 1)
            act.dma_start(a32[:, :], ctxT).then_inc(ev("ctx_loaded"), 16)
            log_gate(0)
            hi(4)
            act.wait_ge(ev("ctx_loaded"), 16)
            for k in range(DC):
                square(a32, k, k)
            hi(4)
            sqrt_stat(D)
            modulated(zhi)
            c.take(tile_read, 4)
            for m in range(DC):
                hi()
                c.take(tile_read)
                act.activation(at(rsil, m), at(rsil, m), ACT.Silu).then_inc(ev("rsil_ready"), 1)
            decays(0)
            hi(4)
            log_gate(1)
            hi(4)
            decays(1)
            hi(4)
            c.take(tile_read, 8)
            for d in range(2):
                if d:
                    act.wait_ge(ev("factors"), 8 + d)
                log_gate(2 + d)
                act.wait_ge(ev("expo"), 9 + d)
                act.activation(a32[:, d * GH * T:(d + 1) * GH * T], za[:, :], ACT.Exp, scale=-INV_TAU if d == 0 else INV_TAU)\
                    .then_inc(ev("factors"), 1)
            for hd in range(GH):
                act.wait_ge(ev("gla_out"), hd + 1)
                act.activation(osq[:, :], ps[5 + hd % 2][:, :], ACT.Square).then_inc(ev("gla_squares"), 1)
                sqrt_stat(2 * P)
                for vc in range(2):
                    c.take(y_f32)
                    c.sig(act.activation(at(zhi, 2 * hd + vc), at(rsil, 2 * hd + vc), ACT.Copy), yhi_ready)
            resid(1, None)
            sqrt_stat(D)
            modulated(xhi)
            with c.loop(MC // 4, {hi_ready: 4, y_f32: 4, yhi_ready: 4}) as i:
                for j in range(4):
                    hi()
                    settled()
                    c.take(y_f32)
                    c.sig(act.activation(at(mhi, i * 4 + j), at(ms, j), ACT.Copy), yhi_ready)
            c.n["tile_read"] += MC

            def mlp_down(first):
                for m in range(2):
                    hi(4)
                    c.take(tile_read)
                    square(h, first + m, m)

            with c.loop(DC // 2 - 1, {hi_ready: 8, tile_read: 2, sq_ready: 2}) as i:
                mlp_down(i * 2)
            mlp_down(DC - 2)
            sqrt_stat(D)

        @block.vector
        def _(dve):
            c = Counts(dve)
            tile = [0]

            def lo(n=1):
                for _ in range(n):
                    u = c.n.get("lo_ready", 0)
                    if u >= UNITS:
                        return
                    w = slice(u % RING * D, (u % RING + 1) * D)
                    c.take(hi_ready)
                    c.sig(dve.tensor_tensor(wlo[:, w], raw[:, w], whi[:, w], ALU.subtract), lo_ready)

            def link(ins):
                c.sig(ins, seq_dve)
                c.again(seq_dve)

            def result(n_units, width=T):
                if n_units:
                    c.take(pe_units, n_units)
                tile[0] += 1
                return ps[(tile[0] - 1) % RING][:, 0:width]

            def add_square(k):
                c.take(sq_ready)
                c.again(ssum_ready)
                c.sig(dve.tensor_tensor(ssum[:, :], ssum[:, :], at(sq, k % 2), ALU.add), ssum_ready)

            def split_lo(k, gain, kk):
                c.take(xhi_ready)
                c.sig(dve.scalar_tensor_tensor(out=at(xlo, k), in0=at(h, k), scalar=gain, in1=at(xhi, k),
                                               op0=ALU.mult, op1=ALU.subtract), x_ready)
                add_square(kk)

            def reciprocal_root(dst):
                c.take(root_ready)
                c.sig(dve.reciprocal(dst[:, :], root[:, :]), rstd_ready)
                c.again(rstd_ready)

            def clear_sum():
                link(dve.memset(ssum[:, :], 0.0))

            def taps(j, w0, w1):
                c.take(tap_ready)
                o = j * (T + 2)
                link(dve.scalar_tensor_tensor(out=at(cv, j), in0=U[:, o + 1:o + T + 1], scalar=w1, in1=at(cv, j),
                                              op0=ALU.mult, op1=ALU.add))
                return dve.scalar_tensor_tensor(out=at(cv, j), in0=U[:, o:o + T], scalar=w0, in1=at(cv, j),
                                                op0=ALU.mult, op1=ALU.add)

            def ffn_up(conv):
                base = VEC[conv][0]
                with c.loop(FC // 2, {hi_ready: 4, lo_ready: 4, pe_units: 4, tile_read: 4, tap_ready: 4,
                                      conv_ready: 4, sil_ready: 2, y_f32: 2, yhi_ready: 2, y_ready: 2,
                                      seq_dve: 4}) as i:
                    def rows(j):
                        lo()
                        c.sig(dve.tensor_tensor(U[:, j * (T + 2) + 2:(j + 1) * (T + 2)], result(1), rstd[:, :],
                                                ALU.mult), tile_read)

                    def conv_of(j):
                        w = i * 12 + (base + 3 * j)
                        c.sig(taps(j, vt[:, bass.ds(w, 1)], vt[:, bass.ds(w + 1, 1)]), conv_ready)

                    def gated(f):
                        c.take(sil_ready)
                        c.again(conv_ready)
                        c.sig(dve.tensor_tensor(at(prod, f), at(sil, f), at(cv, 2 * f + 1), ALU.mult), y_f32)

                    def gated_lo(f):
                        c.take(yhi_ready)
                        c.sig(dve.tensor_tensor(at(ylo, i * 2 + f), at(prod, f), at(yhi, i * 2 + f), ALU.subtract),
                              y_ready)

                    rows(0)
                    rows(1)
                    conv_of(0)
                    rows(2)
                    conv_of(1)
                    gated(0)
                    rows(3)
                    conv_of(2)
                    gated_lo(0)
                    conv_of(3)
                    gated(1)
                    gated_lo(1)

            def resid(units_per, gain, gate=None):
                clear_sum()
                n = 4 * units_per
                per = {hi_ready: n, lo_ready: n, pe_units: n, tile_read: 4, sq_ready: 4, ssum_ready: 4}
                if gain:
                    per |= {xhi_ready: 4, x_ready: 4}
                with c.loop(2, per) as i:
                    def finish(m):
                        if gain:
                            split_lo(i * 4 + m, vt[:, bass.ds(i * 4 + (VEC[gain][0] + m), 1)], m)
                        else:
                            add_square(m)

                    for m in range(4):
                        lo(units_per)
                        r, hm = result(units_per), at(h, i * 4 + m)
                        if gate is None:
                            ins = dve.tensor_tensor(hm, r, hm, ALU.add)
                        else:
                            ins = dve.scalar_tensor_tensor(out=hm, in0=r, scalar=mod[:, bass.ds(i * 4 + (gate + m), 1)],
                                                           in1=hm, op0=ALU.mult, op1=ALU.add)
                        c.sig(ins, tile_read)
                        if m:
                            finish(m - 1)
                    finish(3)

            dve.memset(U[:, :], 0.0).then_inc(ev("pads"), 1)
            clear_sum()
            dve.wait_ge(ev("tables"), 32)
            dve.wait_ge(ev("x_loaded"), 16)
            for k in range(DC):
                split_lo(k, col("g_mix0", k), k)
            lo(LEAD)
            reciprocal_root(rstd)
            dve.wait_ge(ev("pads"), 1)
            with c.loop(2, {hi_ready: 12, lo_ready: 12, pe_units: 12, tile_read: 12, u_ready: 4, tap_ready: 4,
                            y_f32: 4, yhi_ready: 4, y_ready: 4, seq_dve: 8}) as i:
                for j in range(4):
                    lo()
                    c.sig(dve.tensor_tensor(at(sil, 0), result(1), rstd[:, :], ALU.mult), tile_read)
                    lo()
                    c.sig(dve.tensor_tensor(at(sil, 1), result(1), rstd[:, :], ALU.mult), tile_read)
                    c.again(tile_read)
                    c.sig(dve.tensor_tensor(U[:, j * (T + 2) + 2:(j + 1) * (T + 2)], at(sil, 0), at(sil, 1), ALU.mult),
                          u_ready)
                    lo()
                    w = i * 12 + (VEC["conv_mix"][0] + 3 * j)
                    link(taps(j, vt[:, bass.ds(w, 1)], vt[:, bass.ds(w + 1, 1)]))
                    c.sig(dve.tensor_tensor(at(prod, j % 2), result(1), rstd[:, :], ALU.mult), tile_read)
                    c.again(tile_read)
                    c.sig(dve.tensor_tensor(at(prod, j % 2), at(prod, j % 2), at(cv, j), ALU.mult), y_f32)
                    c.take(yhi_ready)
                    c.sig(dve.tensor_tensor(at(ylo, i * 4 + j), at(prod, j % 2), at(yhi, i * 4 + j), ALU.subtract),
                          y_ready)
            resid(1, "g_ffn0")
            reciprocal_root(rstd)

            ffn_up("conv0")
            resid(3, "g_kvin")
            reciprocal_root(rstd)
            for u in range(4):
                lo()
                for k in range(2 * u, 2 * u + 2):
                    c.take(xhi_ready)
                    c.sig(dve.scalar_tensor_tensor(out=at(olo, k), in0=at(h, k), scalar=col("g_mix1", k),
                                                   in1=at(ohi, k), op0=ALU.mult, op1=ALU.subtract), x_ready)
                dst = at(kf, u) if u < RK else at(rt, u - RK)
                c.sig(dve.tensor_tensor(dst, result(1), rstd[:, :], ALU.mult), tile_read)
            dve.wait_ge(ev("tables_late"), 48)
            c.again(tile_read)
            for half, names in enumerate((("cos_a", "sin_a"), ("cos_b", "sin_b"))):
                dve.tensor_tensor(at(rt, 2), at(rt, 0), rot_of(names[0]), ALU.mult)
                link(dve.tensor_tensor(at(rt, 3), at(rt, 1), rot_of(names[1]), ALU.mult))
                link(dve.tensor_tensor(at(kr, half), at(rt, 2), at(rt, 3), ALU.add))
            for j in range(RQ):
                lo()
                c.sig(dve.tensor_tensor(at(cf, j), result(1), rstd[:, :], ALU.mult), tile_read)
            reciprocal_root(rk)
            for k in range(RK):
                last = dve.scalar_tensor_tensor(out=at(kf, k), in0=at(kf, k), scalar=col("g_kv", k), in1=rk[:, :],
                                                op0=ALU.mult, op1=ALU.mult)
            last.then_inc(ev("kv_normed"), 1)
            dve.wait_ge(ev("khi_ready"), 1)
            dve.tensor_tensor(klo[:, :], kf[:, :], khi[:, :], ALU.subtract).then_inc(ev("kv_latent"), 1)
            reciprocal_root(rq)
            for k in range(RQ):
                last = dve.scalar_tensor_tensor(out=at(cf, k), in0=at(cf, k), scalar=col("g_q", k), in1=rq[:, :],
                                                op0=ALU.mult, op1=ALU.mult)
            last.then_inc(ev("q_normed"), 1)
            dve.wait_ge(ev("chi_ready"), 1)
            dve.tensor_tensor(clo[:, :], cf[:, :], chi[:, :], ALU.subtract).then_inc(ev("q_latent"), 1)
            for u in range(2):
                lo()
                for m in range(4):
                    c.sig(dve.tensor_copy(at(kn, 4 * u + m), result(m == 0)), tile_read)
            lo(2)
            for n in range(2):
                for tk in range(2):
                    c.sig(dve.tensor_copy(vv[:, tk * D + n * 512:tk * D + (n + 1) * 512],
                                          result(2 if n + tk == 0 else 0, 512)), tile_read)
            for u in range(4):
                lo()
                for m in range(2):
                    c.sig(dve.tensor_scalar(at(qn, 2 * u + m), result(m == 0), QK_SCALE, None, ALU.mult), tile_read)
            for u in range(4):
                lo()
                for m in range(2):
                    c.sig(dve.tensor_scalar(at(rt, m), result(m == 0), QK_SCALE, None, ALU.mult), tile_read)
                c.again(tile_read)
                dve.tensor_tensor(at(rt, 2), at(rt, 0), rot_of("cos_q"), ALU.mult)
                link(dve.tensor_tensor(at(rt, 3), at(rt, 1), rot_of("sin_q"), ALU.mult))
                dve.tensor_tensor(at(qr, u), at(rt, 2), at(rt, 3), ALU.add).then_inc(ev("queries"), 1)
                dve.wait_ge(ev("queries"), u + 1)
            for hd in range(HEADS + 2):
                if hd < HEADS:
                    s0, m0 = hd % 2 * 3 * P, hd % 2 * 8
                    dve.wait_ge(ev("scores"), hd + 1)
                    if hd >= 2:
                        dve.wait_ge(ev("turned"), hd - 1)
                    dve.tensor_tensor(sm[:, s0:s0 + 3 * P], ps[hd % 2][:, 0:3 * P], rot_of("mask_s"), ALU.add)\
                        .then_inc(ev("masked"), 1)
                    dve.wait_ge(ev("masked"), hd + 1)
                    dve.tensor_reduce(mx[:, m0:m0 + 1], sm[:, s0:s0 + P], AX.X, ALU.max)
                    link(dve.tensor_reduce(mx[:, m0 + 1:m0 + 2], sm[:, s0 + P:s0 + 3 * P], AX.X, ALU.max))
                    dve.tensor_scalar(mx[:, m0 + 2:m0 + 4], mx[:, m0:m0 + 2], -1.0, None, ALU.mult)\
                        .then_inc(ev("negmax"), 1)
                if 1 <= hd <= HEADS:
                    g = hd - 1
                    s0, m0 = g % 2 * 3 * P, g % 2 * 8
                    dve.wait_ge(ev("exps"), g + 1)
                    link(dve.reciprocal(mx[:, m0 + 6:m0 + 8], mx[:, m0 + 4:m0 + 6]))
                    dve.tensor_scalar(sm[:, s0:s0 + P], sm[:, s0:s0 + P], mx[:, m0 + 6:m0 + 7], None, ALU.mult)
                    dve.tensor_scalar(sm[:, s0 + P:s0 + 3 * P], sm[:, s0 + P:s0 + 3 * P], mx[:, m0 + 7:m0 + 8], None,
                                      ALU.mult).then_inc(ev("weights"), 1)
                if hd >= 2:
                    g = hd - 2
                    c.take(xhi_ready)
                    c.sig(dve.tensor_tensor(at(olo, g), ps[5 + g % 2][:, 0:T], at(ohi, g), ALU.subtract), x_ready)
            resid(1, "g_ffn1")
            reciprocal_root(rstd)
            pads = U[:, :].rearrange("p (j t) -> p j t", t=T + 2)[:, :, 0:2]
            link(dve.memset(pads, 0.0))
            ffn_up("conv1")
            resid(3, None)

            def modulated(src, g0, s0, lo_dst):
                for k in range(DC + 2):
                    if k < DC:
                        c.sig(dve.scalar_tensor_tensor(out=at(a32, k), in0=at(src, k), scalar=gmod[:, g0 + k:g0 + k + 1],
                                                       in1=rstd[:, :], op0=ALU.mult, op1=ALU.mult), seq_dve)
                    if 1 <= k <= DC:
                        c.again(seq_dve, 1 if k < DC else 0)
                        c.sig(dve.tensor_scalar(at(a32, k - 1), at(a32, k - 1), mod[:, s0 + k - 1:s0 + k], None, ALU.add),
                              a_ready)
                    if k >= 2:
                        c.take(xhi_ready)
                        c.sig(dve.tensor_tensor(at(lo_dst, k - 2), at(a32, k - 2), at(xhi if lo_dst is xlo else zhi, k - 2),
                                                ALU.subtract), x_ready)

            def by_head(t, w=T):
                return t[:, :].rearrange("p (m t) -> p m t", t=w)

            def border(first, step, n, width):
                v = by_head(pb, T + 1)[:, :, first:first + step * (n - 1) + 1:step]
                return v.unsqueeze(3).to_broadcast([P, GH, n, width])

            def one_border(first):
                return by_head(pb, T + 1)[:, :, first:first + 1].to_broadcast([P, GH, T])

            def log_decay(i, bank0=5):
                dve.wait_ge(ev("gate_abs"), i + 1)
                for m in range(GH):
                    last = dve.tensor_scalar(at(zm, m), ps[bank0 + m // 2][:, m % 2 * T:(m % 2 + 1) * T],
                                             col("b_gate", i % 2 * GH + m), 0.0, ALU.add, ALU.min)
                last.then_inc(ev("gate_read"), 1)
                dve.wait_ge(ev("gate_read"), i + 1)
                dve.wait_ge(ev("gate_ln"), i + 1)
                link(dve.tensor_tensor(zm[:, :], zm[:, :], za[:, :], ALU.subtract))
                for m in range(GH):
                    last = dve.tensor_tensor_scan(out=pb[:, m * (T + 1) + 1:(m + 1) * (T + 1)], data0=one_t[:, :],
                                                  data1=at(zm, m), initial=0.0, op0=ALU.mult, op1=ALU.add)
                link(last)

            def chunks(t, n, w):
                return t.rearrange("p (m c t) -> p m c t", m=GH, c=n)

            def decays(d):
                n = 4 * d
                sums = by_head(pb, T + 1)[:, :, 1 - d:T + 1 - d]
                by_chunk = sums.rearrange("p m (c t) -> p m c t", t=CH)
                dve.tensor_tensor(chunks(za[:, :], 4, CH), by_chunk, border(CH * d, CH, 4, CH), ALU.subtract)\
                    .then_inc(ev("expo"), 1)
                dve.tensor_tensor(by_head(zm), sums, one_border(P), ALU.subtract)\
                    .then_inc(ev("expo"), 1)
                dve.wait_ge(ev("factors"), n + 1)
                dve.tensor_tensor(chunks(za[:, 0:GH * 2 * CH], 2, CH), by_chunk[:, :, d::2, :],
                                  border(CH, P, 2, CH), ALU.subtract).then_inc(ev("expo"), 1)
                dve.tensor_tensor(qd[d][:, :], qd[d][:, :], gq[:, :], ALU.mult)
                dve.tensor_tensor(ki[d][:, :], ki[d][:, :], gk[:, :], ALU.mult)
                dve.wait_ge(ev("factors"), n + 2)
                if d == 0:
                    dve.tensor_copy(by_head(zm), sums).then_inc(ev("expo"), 1)
                else:
                    dve.tensor_tensor(by_head(zm), sums, one_border(T),
                                      ALU.subtract).then_inc(ev("expo"), 1)
                first, second = (gk, gq) if d == 0 else (gq, gk)
                dve.tensor_tensor(by_head(qk[d])[:, :, 0:P], by_head(qk[d])[:, :, 0:P], by_head(first)[:, :, 0:P], ALU.mult)
                dve.tensor_tensor(by_head(qk[d])[:, :, P:T], by_head(qk[d])[:, :, P:T], by_head(second)[:, :, P:T], ALU.mult)
                dve.wait_ge(ev("factors"), n + 3)
                dve.tensor_tensor(chunks(kw[d][:, :], 2, CH), chunks(kw[d][:, :], 2, CH),
                                  chunks(gk[:, :], 4, CH)[:, :, d::2, :], ALU.mult)
                dve.wait_ge(ev("factors"), n + 4)
                dve.tensor_tensor(qf[d][:, :], qf[d][:, :], gq[:, :], ALU.mult).then_inc(ev("decayed"), 1)

            dve.wait_ge(ev("ada_summed"), 8)
            b_ada = VEC["b_ada"][0]
            dve.tensor_tensor(mod[:, 0:48], ps[7][:, 0:48], vt[:, b_ada:b_ada + 48], ALU.add)
            link(dve.tensor_tensor(mod[:, 48:64], ps[7][:, 48:64], vt[:, b_ada:b_ada + 16], ALU.add))
            for n, (scale, gain) in enumerate(((8, "g_n1"), (32, "g_n2"), (56, "g_n1"))):
                link(dve.scalar_tensor_tensor(out=gmod[:, n * DC:(n + 1) * DC], in0=mod[:, scale:scale + DC], scalar=1.0,
                                              in1=vt[:, VEC[gain][0]:VEC[gain][0] + DC], op0=ALU.add, op1=ALU.mult))
            reciprocal_root(rstd)
            clear_sum()
            for k in range(DC):
                dve.scalar_tensor_tensor(out=at(h, k), in0=at(h, k), scalar=col("g_fin1", k), in1=rstd[:, :],
                                         op0=ALU.mult, op1=ALU.mult).then_inc(ev("fin_ready"), 1)
            for k in range(DC):
                add_square(k)
            reciprocal_root(rstd)
            modulated(h, 0, 0, xlo)
            dve.memset(one_t[:, :], 1.0)
            link(dve.memset(pb[:, :], 0.0))
            for m in range(GH):
                lo()
                c.sig(dve.tensor_scalar(at(gq, m), result(1), GLA_SCALE, None, ALU.mult), tile_read)
            for m in range(GH):
                lo()
                c.sig(dve.tensor_copy(at(gk, m), result(1)), tile_read)
            dve.wait_ge(ev("gate_in"), 1)
            dve.tensor_copy(t1[:, :], ps[7][0:32, 0:T]).then_inc(ev("gate_in_read"), 1)
            clear_sum()
            lo(4)
            log_decay(0)
            for k in range(DC):
                add_square(k)
            lo(4)
            for n in range(2):
                for tk in range(2):
                    c.sig(dve.tensor_copy(gv[:, tk * D + n * 512:tk * D + (n + 1) * 512],
                                          result(8 if n + tk == 0 else 0, 512)), tile_read)
            reciprocal_root(rstd)
            modulated(a32, 2 * DC, 6 * DC, zlo)
            for m in range(DC):
                lo()
                c.sig(dve.tensor_copy(at(rsil, m), result(1)), tile_read)
            decays(0)
            for m in range(GH):
                lo()
                c.sig(dve.tensor_copy(at(ck, m), result(1)), tile_read)
            log_decay(1)
            dve.wait_ge(ev("gate_in"), 2)
            dve.wait_ge(ev("gate_out"), 2)
            dve.tensor_copy(t1[:, :], ps[7][0:32, 0:T]).then_inc(ev("gate_in_read"), 1)
            lo(4)
            decays(1)
            lo(4)
            for n in range(2):
                for tk in range(2):
                    c.sig(dve.tensor_copy(cval[:, tk * D + n * 512:tk * D + (n + 1) * 512],
                                          result(8 if n + tk == 0 else 0, 512)), tile_read)
            for d in range(2):
                log_decay(2 + d)
                sums = by_head(pb, T + 1)[:, :, 1 - d:T + 1 - d]
                dve.tensor_tensor(by_head(za), sums, one_border(T if d == 0 else 0),
                                  ALU.subtract).then_inc(ev("expo"), 1)
                w = slice(d * GH * T, (d + 1) * GH * T)
                dve.wait_ge(ev("factors"), 9 + d)
                dve.tensor_tensor(a32[:, w], a32[:, w], ck[:, :], ALU.mult).then_inc(ev("ctx_decayed"), 1)
                for tk in range(2):
                    dve.wait_ge(ev("ctx_turned"), 2 * d + tk + 1)
                    if d:
                        dve.wait_ge(ev("state_out"), 1)
                    dve.tensor_copy(kt[:, tk * GH * P:(tk + 1) * GH * P], ps[7][:, :]).then_inc(ev("ctx_turned_read"), 1)
                dve.wait_ge(ev("state_out"), d + 1)
                dve.tensor_copy(state[:, w.start:w.start + 512], ps[2 * d][:, :])
                dve.tensor_copy(state[:, w.start + 512:w.stop], ps[2 * d + 1][:, :]).then_inc(ev("state_read"), 1)

            def gla_mask(n):
                dve.wait_ge(ev("gla_scores"), n + 1)
                if n >= 4:
                    dve.wait_ge(ev("gla_out"), n // 2 - 1)
                dve.tensor_tensor(att[:, n % 4 * 3 * P:(n % 4 + 1) * 3 * P], ps[n % 4][:, 0:3 * P],
                                  cst_of("mask_b" if n % 2 else "mask_f"), ALU.mult).then_inc(ev("gla_masked"), 1)

            for n in range(4):
                gla_mask(n)
            for hd in range(GH):
                if hd + 2 < GH:
                    gla_mask(2 * hd + 4)
                    gla_mask(2 * hd + 5)
                reciprocal_root(rstd)
                for vc in range(2):
                    k = 2 * hd + vc
                    tmp = at(zm, vc)
                    ins = dve.scalar_tensor_tensor(out=tmp, in0=ps[5 + hd % 2][:, vc * T:(vc + 1) * T],
                                                   scalar=col("g_head", k), in1=rstd[:, :], op0=ALU.mult, op1=ALU.mult)
                    if vc == 1:
                        ins.then_inc(ev("gla_read"), 1)
                        dve.wait_ge(ev("gla_read"), hd + 1)
                    else:
                        link(ins)
                    dve.wait_ge(ev("rsil_ready"), k + 1)
                    c.sig(dve.tensor_tensor(at(rsil, k), at(rsil, k), tmp, ALU.mult), y_f32)
                for vc in range(2):
                    k = 2 * hd + vc
                    c.take(yhi_ready)
                    c.sig(dve.tensor_tensor(at(zlo, k), at(rsil, k), at(zhi, k), ALU.subtract), y_ready)
            resid(1, None, gate=2 * DC)
            reciprocal_root(rstd)
            modulated(h, DC, 3 * DC, xlo)
            with c.loop(MC // 4, {hi_ready: 4, lo_ready: 4, pe_units: 4, tile_read: 4, y_f32: 4, yhi_ready: 4,
                                  y_ready: 4}) as i:
                def inner_lo(j):
                    c.take(yhi_ready)
                    c.sig(dve.tensor_tensor(at(mlo, i * 4 + j), at(ms, j), at(mhi, i * 4 + j), ALU.subtract), y_ready)

                for j in range(4):
                    lo()
                    c.sig(dve.tensor_scalar(at(mr, j), result(1), 0.0, None, ALU.max), tile_read)
                    c.again(tile_read)
                    c.sig(dve.tensor_tensor(at(ms, j), at(mr, j), at(mr, j), ALU.mult), y_f32)
                    if j:
                        inner_lo(j - 1)
                inner_lo(3)
            clear_sum()

            def mlp_down(first):
                for m in range(2):
                    lo(4)
                    c.take(pe_units, 4)
                    hm = at(h, first + m)
                    c.sig(dve.scalar_tensor_tensor(out=hm, in0=ps[m][:, 0:T],
                                                   scalar=mod[:, 5 * DC + first + m:5 * DC + first + m + 1]
                                                   if isinstance(first, int) else mod[:, bass.ds(first + (5 * DC + m), 1)],
                                                   in1=hm, op0=ALU.mult, op1=ALU.add), tile_read)
                    add_square(m)

            with c.loop(DC // 2 - 1, {hi_ready: 8, lo_ready: 8, pe_units: 8, tile_read: 2, sq_ready: 2,
                                      ssum_ready: 2}) as i:
                mlp_down(i * 2)
            mlp_down(DC - 2)
            reciprocal_root(rstd)
            for k in range(DC):
                dve.scalar_tensor_tensor(out=at(h, k), in0=at(h, k), scalar=col("g_fin2", k), in1=rstd[:, :],
                                         op0=ALU.mult, op1=ALU.mult).then_inc(ev("out_chunk"), 1)


def columns(v, n):
    return v.reshape(n, P).T


def feature_major(x):
    return x.T.reshape(DC, P, T).transpose(1, 0, 2).reshape(P, DC * T)


def tiles(w, order=None, pad=0):
    K, M = w.shape[0] // P, w.shape[1] // P
    b = w.reshape(K, P, M, P).transpose(2, 0, 1, 3)
    if order is not None:
        b = b[order]
    if pad:
        b = np.concatenate([b, np.zeros((M, pad, P, P), w.dtype)], 1)
    return b.reshape(-1, P, P)


def wide(w):
    K, M = w.shape[0] // P, w.shape[1] // 512
    return w.reshape(K, P, M, 4, P).transpose(2, 0, 3, 1, 4).reshape(-1, P, P)


def lay_out(a):
    gu = np.stack([np.arange(FC), FC + np.arange(FC)], 1).reshape(-1)
    chb = np.stack([DC + np.arange(DC), 2 * DC + np.arange(DC), np.arange(DC)], 1).reshape(-1)
    dkv = a["w_dkv"]
    rot = dkv[:, 256:320]
    swap = np.concatenate([rot[:, 32:], rot[:, :32]], 1)
    dkv = np.concatenate([dkv[:, :256], rot, rot, swap, swap], 1)
    ukv = a["w_ukv"].reshape(256, HEADS, 2, P)
    uq = a["b_w_uq"][0].reshape(512, HEADS, 192)
    qrot = uq[:, :, 128:]
    qswap = np.concatenate([qrot[..., 32:], qrot[..., :32]], -1)
    q_pairs = np.stack([qrot.reshape(512, HP, P), qswap.reshape(512, HP, P)], 2).reshape(512, 2 * HP * P)
    win = a["gla_w_in_2"][0]
    gla = {"q": win[:, 0:512], "k": win[:, 512:1024], "v": win[:, 1024:2048], "r": win[:, 2048:3072]}
    parts = [
        tiles(a["a_w_in"][0], chb), tiles(a["a_w_out"][0]),
        tiles(a["ffn_w_up"][0], gu), tiles(a["ffn_w_down"][0], pad=2),
        tiles(dkv), tiles(a["b_w_dq"][0]),
        tiles(np.ascontiguousarray(ukv[:, :, 0]).reshape(256, D)),
        ukv[:, :, 1].reshape(2, P, 8, P).transpose(0, 2, 1, 3).reshape(-1, P, P),
        tiles(np.ascontiguousarray(uq[:, :, :128]).reshape(512, D)), tiles(q_pairs),
        tiles(a["b_w_o"][0]), tiles(a["ffn_w_up"][1], gu), tiles(a["ffn_w_down"][1], pad=2),
        tiles(gla["q"]), tiles(gla["k"]), wide(gla["v"]), tiles(gla["r"]),
        tiles(gla["k"]), wide(gla["v"]),
        tiles(a["gla_w_o_2"][0]), tiles(a["mlp_w1_2"][0]), tiles(a["mlp_w2_2"][0]),
    ]
    blocks = np.concatenate(parts)
    stream = np.ascontiguousarray(blocks.reshape(UNITS, BLK, P, P).transpose(0, 2, 1, 3)).reshape(UNITS, P, D)

    def conv(w, order):
        n = w.shape[1] // P
        return w.reshape(3, n, P)[:, order].transpose(2, 1, 0).reshape(P, 3 * n)

    vec = np.concatenate([
        columns(a["a_mix_norm"][0], 8), columns(a["ffn_norm"][0], 8), columns(a["kv_in_norm"], 8),
        columns(a["b_mix_norm"][0], 8), columns(a["b_q_norm"][0], 4), columns(a["kv_norm"], 2),
        columns(a["ffn_norm"][1], 8), columns(a["final_norm"], 8), columns(a["norm1_g_2"][0], 8),
        columns(a["norm2_g_2"][0], 8), columns(a["final_g_2"], 8), columns(a["gla_g_head_2"][0].reshape(-1), 8),
        columns(a["gla_b_a_2"][0].reshape(-1), 8), columns(a["ada_b_2"][0], 48), columns(a["c_2"][0], 8),
        columns(a["c_ctx_2"], 8), conv(a["a_conv"][0], np.arange(DC)), conv(a["ffn_conv"][0], gu),
        conv(a["ffn_conv"][1], gu)], 1)

    row, colm = np.arange(P)[:, None], np.arange(P)[None, :]
    one = np.ones((P, P), np.float32)
    hidden = np.where(colm <= row, 0.0, -1e30)
    upper, lower = (row <= colm) * one, (row >= colm) * one
    cst = np.concatenate([one, np.eye(P), upper, one, upper, lower, one, lower], 1).astype(np.float32)
    inv = (1.0 / (np.float32(10000.0) ** (np.arange(0, 64, 2, dtype=np.float32) / np.float32(64)))).astype(np.float32)
    ang = (np.arange(T, dtype=np.float32)[None, :] * inv[:, None]).astype(np.float32)
    cos = np.concatenate([np.cos(ang)] * 2)
    sin = np.concatenate([-np.sin(ang), np.sin(ang)])
    none = np.zeros((64, T), np.float32)
    rotary = np.concatenate([hidden, 0 * one, hidden] + [np.concatenate(p) for p in (
        (cos, cos), (sin, sin), (cos, none), (sin, none), (none, cos), (none, sin))], 1).astype(np.float32)

    wa1 = np.concatenate(list(a["gla_w_a1_2"][0]), 1).reshape(DC, P, 32).transpose(1, 0, 2).reshape(P, DC * 32)
    w2 = a["gla_w_a2_2"][0]
    wa2 = np.zeros((32, D), w2.dtype)
    wa2[0:16, 0:512], wa2[16:32, 512:1024] = w2[0], w2[1]
    ada = a["ada_w_2"][0].reshape(DC, P, 6, D).transpose(2, 0, 1, 3).reshape(6 * DC, P, D)
    return {"stream": stream, "xT": feature_major(a["x"][0]), "ctxT": feature_major(a["ctx_2"][0]), "vec": vec,
            "cst": cst, "rot": rotary, "wa1": wa1, "wa2": wa2, "ada": ada}


def kernel(**inputs):
    import concourse.bacc as bacc
    from concourse.bass_utils import run_bass_kernel_spmd

    arrays = {k: np.ascontiguousarray(v) for k, v in lay_out({k: np.asarray(v) for k, v in inputs.items()}).items()}
    nc = bacc.Bacc("TRN2", target_bir_lowering=False, num_devices=1)
    args = [nc.dram_tensor(k, v.shape, F32, kind="ExternalInput").ap() for k, v in arrays.items()]
    out = nc.dram_tensor("out", (P, DC * T), F32, kind="ExternalOutput").ap()
    program(nc, *args, out)
    got = run_bass_kernel_spmd(nc, [arrays], core_ids=[0]).results[0]["out"]
    return got.reshape(P, DC, T).transpose(1, 0, 2).reshape(D, T).T.reshape(1, T, D)
```

```python
from contextlib import ExitStack, contextmanager

import numpy as np

import concourse.bass as bass
from concourse import mybir

F32 = mybir.dt.float32
F32R = mybir.dt.float32r
ALU = mybir.AluOpType
ACT = mybir.ActivationFunctionType
AX = mybir.AxisListType

P = 128
T = 256
D = 1024
DC = D // P
FF = 2816
FC = FF // P
HEADS = 8
HP = HEADS // 2
RQ = 512 // P
RK = 256 // P
GH = 4
CH = 64
MC = 4096 // P
EPS = 1e-6
QK_SCALE = (128 + 64) ** -0.5
GLA_SCALE = 128 ** -0.5
INV_TAU = 1.0 / 16.0
RING = 4
LEAD = 3
BLK = 8

PHASES = [("mix_in", 3 * DC), ("mix_out", DC), ("up0", 2 * FC), ("down0", 3 * DC), ("dkv", 4), ("dq", 4),
          ("ukv", 4), ("uq", 8), ("attn_out", DC), ("up1", 2 * FC), ("down1", 3 * DC),
          ("gla_q", 4), ("gla_k", 4), ("gla_v", 8), ("gla_r", 8), ("ctx_k", 4), ("ctx_v", 8),
          ("gla_out", DC), ("mlp_up", MC), ("mlp_down", MC)]
UNITS = sum(n for _, n in PHASES)
ADA_JOBS = [(0, ((0, False), (1, True)), 0), (2, ((0, False),), 2), (3, ((1, False),), 2), (4, ((0, False),), 3),
            (5, ((1, False),), 4), (1, ((0, False),), 5), (1, ((1, True),), 6)]
OWN_GROUPS = 4
PHASE_AT = {name: sum(n for _, n in PHASES[:i]) for i, (name, _) in enumerate(PHASES)}
assert PHASE_AT["up0"] % RING == 0 and PHASE_AT["up1"] % RING == 0 and LEAD == RING - 1

VEC = {}
for _name, _n in [("g_mix0", 8), ("g_ffn0", 8), ("g_kvin", 8), ("g_mix1", 8), ("g_q", 4), ("g_kv", 2),
                  ("g_ffn1", 8), ("g_fin1", 8), ("g_n1", 8), ("g_n2", 8), ("g_fin2", 8), ("g_head", 8),
                  ("b_gate", 8), ("b_ada", 48), ("c", 8), ("c_ctx", 8), ("conv_mix", 3 * DC),
                  ("conv0", 3 * 2 * FC), ("conv1", 3 * 2 * FC)]:
    VEC[_name] = sum(n for _, n in VEC.values()), _n
NVEC = sum(n for _, n in VEC.values())

CST = {}
for _name, _n in [("ones", P), ("ident", P), ("mask_f", 3 * P), ("mask_b", 3 * P)]:
    CST[_name] = sum(n for _, n in CST.values()), _n
NCST = sum(n for _, n in CST.values())
ROT = {}
for _name, _n in [("mask_s", 3 * P), ("cos_q", T), ("sin_q", T), ("cos_a", T), ("sin_a", T), ("cos_b", T), ("sin_b", T)]:
    ROT[_name] = sum(n for _, n in ROT.values()), _n
NROT = sum(n for _, n in ROT.values())


class Counts:

    def __init__(self, eng):
        self.eng, self.n, self.i, self.per, self.start = eng, {}, None, {}, {}

    def value(self, sem, extra=0):
        n = self.n.get(sem.name, 0) + extra
        if self.i is None or not self.per.get(sem.name):
            return n
        return self.i * self.per[sem.name] + n

    def slot_value(self, u):
        n = u // RING + 1
        if self.i is None or not self.per.get("unit"):
            return n
        return self.i * (self.per["unit"] // RING) + n

    def take(self, sem, by=1):
        self.n[sem.name] = self.n.get(sem.name, 0) + by
        self.eng.wait_ge(sem, self.value(sem))

    def sig(self, ins, sem, by=1):
        self.n[sem.name] = self.n.get(sem.name, 0) + by
        ins.then_inc(sem, by)

    def again(self, sem, back=0):
        if self.n.get(sem.name, 0) - back > 0:
            self.eng.wait_ge(sem, self.value(sem, -back))

    @contextmanager
    def loop(self, times, per):
        with self.eng.Fori(0, times) as i:
            self.i, self.start = i, dict(self.n)
            self.per = {s if s == "unit" else s.name: k for s, k in per.items()}
            yield i
        for name in {*self.n, *self.per}:
            k = self.n.get(name, 0) - self.start.get(name, 0)
            assert k == self.per.get(name, 0), (name, k, self.per.get(name, 0))
            self.n[name] = self.start.get(name, 0) + k * times
        self.i, self.per = None, {}


def at(t, k):
    return t[:, k * T:(k + 1) * T] if isinstance(k, int) else t[:, bass.ds(k * T, T)]


def program(nc, stream, xT, ctxT, vec, cst, rot, wa1, wa2, ada, out):
    ctx = ExitStack()

    def sb(name, cols, dt=F32, stack=ctx, rows=P):
        return stack.enter_context(nc.sbuf_tensor(name, [rows, cols], dt))

    with ctx:
        raw = sb("raw", RING * D)
        whi = sb("whi", RING * D, F32R)
        wlo = sb("wlo", RING * D, F32R)
        h = sb("h", DC * T)
        vt = sb("vt", NVEC)
        ct = sb("ct", NCST)
        wa1s = sb("wa1s", DC * 32)
        wa2s = sb("wa2s", D, rows=32)
        rstd = sb("rstd", T)
        root = sb("root", T)
        ssum = sb("ssum", 2 * T)
        sq = sb("sq", 2 * T)
        mod = sb("mod", 64)
        gmod = sb("gmod", 3 * DC)
        sc = sb("sc", 16)
        state = sb("state", 2 * GH * T)
        stage = ExitStack()
        xhi = sb("xhi", DC * T, F32R, stage)
        xlo = sb("xlo", DC * T, F32R, stage)
        stage.close()
        stage = ExitStack()
        ck = sb("ck", GH * T, F32, stage)
        cval = sb("cval", 2 * D, F32, stage)
        kt = sb("kt", 2 * GH * P, F32, stage)
        stage.close()
        sb("x_held", 2 * DC * T)
        stage = ExitStack()
        yhi = sb("yhi", FC * T, F32R, stage)
        ylo = sb("ylo", FC * T, F32R, stage)
        U = sb("U", 4 * (T + 2), F32, stage)
        cv = sb("cv", 4 * T, F32, stage)
        sil = sb("sil", 2 * T, F32, stage)
        prod = sb("prod", 2 * T, F32, stage)
        stage.close()
        EARLY = 2 * HEADS * T + HEADS * T + HP * T + HEADS * T + 2 * T + 2 * D + 4 * RQ * T + 4 * RK * T + 6 * T + 3 * 3 * P + 24
        stage = ExitStack()
        ohi = sb("ohi", HEADS * T, F32R, stage)
        olo = sb("olo", HEADS * T, F32R, stage)
        qn = sb("qn", HEADS * T, F32, stage)
        qr = sb("qr", HP * T, F32, stage)
        kn = sb("kn", HEADS * T, F32, stage)
        kr = sb("kr", 2 * T, F32, stage)
        vv = sb("vv", 2 * D, F32, stage)
        cf = sb("cf", RQ * T, F32, stage)
        chi = sb("chi", RQ * T, F32R, stage)
        clo = sb("clo", RQ * T, F32R, stage)
        later = ExitStack()
        pt = sb("pt", 2 * 3 * P, F32, later)
        later.close()
        csq = sb("csq", RQ * T, F32, stage)
        kf = sb("kf", RK * T, F32, stage)
        khi = sb("khi", RK * T, F32R, stage)
        klo = sb("klo", RK * T, F32R, stage)
        ksq = sb("ksq", RK * T, F32, stage)
        rk = sb("rk", T, F32, stage)
        rq = sb("rq", T, F32, stage)
        rt = sb("rt", 4 * T, F32, stage)
        sm = sb("sm", 3 * 3 * P, F32, stage)
        mx = sb("mx", 3 * 8, F32, stage)
        stage.close()
        stage = ExitStack()
        sb("stacks_held", EARLY, F32, stage)
        rt_tab = sb("rt_tab", NROT, F32, stage)
        ada_w = sb("ada_w", 2 * D, F32, stage)
        ada_p = sb("ada_p", D, F32, stage)
        ada_acc = sb("ada_acc", 2 * D, F32, stage)
        stage.close()
        stage = ExitStack()
        zhi = sb("zhi", DC * T, F32R, stage)
        zlo = sb("zlo", DC * T, F32R, stage)
        a32 = sb("a32", DC * T, F32, stage)
        gq = sb("gq", GH * T, F32, stage)
        gk = sb("gk", GH * T, F32, stage)
        gv = sb("gv", 2 * D, F32, stage)
        rsil = sb("rsil", DC * T, F32, stage)
        t1 = sb("t1", T, F32, stage, rows=32)
        za = sb("za", GH * T, F32, stage)
        zm = sb("zm", GH * T, F32, stage)
        pb = sb("pb", GH * (T + 1), F32, stage)
        one_t = sb("one_t", T, F32, stage)
        qd = [sb(f"qd{d}", GH * T, F32, stage) for d in range(2)]
        ki = [sb(f"ki{d}", GH * T, F32, stage) for d in range(2)]
        kw = [sb(f"kw{d}", GH * 2 * CH, F32, stage) for d in range(2)]
        qk = [sb(f"qk{d}", GH * T, F32, stage) for d in range(2)]
        qf = [sb(f"qf{d}", GH * T, F32, stage) for d in range(2)]
        att = sb("att", 4 * 3 * P, F32, stage)
        osq = sb("osq", 2 * T, F32, stage)
        stage.close()
        stage = ExitStack()
        mhi = sb("mhi", MC * T, F32R, stage)
        mlo = sb("mlo", MC * T, F32R, stage)
        mr = sb("mr", 4 * T, F32, stage)
        ms = sb("ms", 4 * T, F32, stage)
        stage.close()
        ps = [ctx.enter_context(nc.psum_tensor(f"ps{i}", [P, 512], F32)) for i in range(8)]
        STAT = ps[4]

        named = {}

        def ev(name):
            if name not in named:
                named[name] = ctx.enter_context(nc.semaphore(name))
            return named[name]

        raw_ready = [ev(f"raw_ready{i}") for i in range(RING)]
        hi_ready = ev("hi_ready")
        lo_ready = [ev(f"lo_ready{i}") for i in range(RING)]
        pe_units = ev("pe_units")
        tile_read = ev("tile_read")
        xhi_ready = ev("xhi_ready")
        x_ready = ev("x_ready")
        sq_ready = ev("sq_ready")
        ssum_ready = ev("ssum_ready")
        stat_ready = ev("stat_ready")
        root_ready = ev("root_ready")
        rstd_ready = ev("rstd_ready")
        u_ready = ev("u_ready")
        tap_ready = ev("tap_ready")
        conv_ready = ev("conv_ready")
        sil_ready = ev("sil_ready")
        y_f32 = ev("y_f32")
        yhi_ready = ev("yhi_ready")
        y_ready = ev("y_ready")
        a_ready = ev("a_ready")
        seq_dve = ev("seq_dve")

        def col(name, k=0):
            return vt[:, VEC[name][0] + k:VEC[name][0] + k + 1]

        def vt_col(k):
            return vt[:, k:k + 1] if isinstance(k, int) else vt[:, bass.ds(k, 1)]

        def cst_of(name):
            return ct[:, CST[name][0]:CST[name][0] + CST[name][1]]

        def rot_of(name):
            return rt_tab[:, ROT[name][0]:ROT[name][0] + ROT[name][1]]

        ones, ident = cst_of("ones"), cst_of("ident")
        block = ctx.enter_context(nc.Block())

        @block.sync
        def _(sp):
            def load_group(first, done):
                for j in range(RING):
                    if done is not None:
                        sp.wait_ge(lo_ready[j], done)
                    sp.dma_start(raw[:, j * D:(j + 1) * D], stream[first + j]).then_inc(raw_ready[j], 16)

            sp.dma_start(h[:, :], xT).then_inc(ev("x_loaded"), 16)
            sp.dma_start(vt[:, :], vec).then_inc(ev("tables"), 16)
            sp.dma_start(ct[:, :], cst).then_inc(ev("tables"), 16)
            load_group(0, None)
            sp.dma_start(wa1s[:, :], wa1).then_inc(ev("tables_late"), 16)
            sp.dma_start(wa2s[:, :], wa2).then_inc(ev("tables_late"), 16)
            sp.dma_start(rt_tab[:, :], rot).then_inc(ev("tables_late"), 16)
            with sp.Fori(0, UNITS // RING - 1) as g:
                load_group(g * RING + RING, g + 1)
            for k in range(DC):
                sp.wait_ge(ev("out_chunk"), k + 1)
                sp.dma_start(out[:, k * T:(k + 1) * T], at(h, k)).then_inc(ev("stored"), 16)
            sp.wait_ge(ev("stored"), 16 * DC)

        @block.gpsimd
        def _(pool):
            c = Counts(pool)
            added = ev("ada_added")

            def weighted(b, scalar, acc):
                dst = ada_acc[:, acc * D:(acc + 1) * D]
                pool.wait_ge(ev("sc_ready"), 1)
                c.sig(pool.tensor_tensor(ada_p[:, :], ada_w[:, b * D:(b + 1) * D], scalar.to_broadcast([P, D]),
                                         ALU.mult), added)
                c.again(added)
                c.sig(pool.tensor_tensor(dst, dst, ada_p[:, :], ALU.add), added)
                c.again(added)

            def split_beside_vector(first, groups):
                slot = slice((RING - 1) * D, RING * D)
                c.n["hi_ready"] = first + RING * (FC // 2 - groups)
                with c.loop(groups, {hi_ready: RING}):
                    c.take(hi_ready, RING)
                    pool.tensor_tensor(wlo[:, slot], raw[:, slot], whi[:, slot], ALU.subtract)\
                        .then_inc(lo_ready[RING - 1], 1)

            pool.wait_ge(ev("sc_ready"), 1)
            for job, (s, sums, read) in enumerate(ADA_JOBS):
                if job == 1:
                    split_beside_vector(PHASE_AT["up0"], FC // 2)
                if job == len(ADA_JOBS) - 1:
                    split_beside_vector(PHASE_AT["up1"], FC // 2 - OWN_GROUPS)
                c.again(added)
                for b in range(2):
                    pool.dma_start(ada_w[:, b * D:(b + 1) * D], ada[s * DC + b]).then_inc(ev(f"ada_ready{b}"), 16)
                if read:
                    pool.wait_ge(ev("ada_summed"), read)
                for acc, _ in sums:
                    c.sig(pool.memset(ada_acc[:, acc * D:(acc + 1) * D], 0.0), added)
                c.again(added)

                def two_rows(k, last):
                    for b in range(2):
                        c.take(ev(f"ada_ready{b}"), 16)
                        for acc, of_context in sums:
                            j = k + (b + (DC if of_context else 0))
                            weighted(b, sc[:, j:j + 1] if isinstance(j, int) else sc[:, bass.ds(j, 1)], acc)
                        if not last:
                            pool.wait_ge(ev("sc_ready"), 1)
                            pool.dma_start(ada_w[:, b * D:(b + 1) * D], ada[k + (s * DC + b + 2)])\
                                .then_inc(ev(f"ada_ready{b}"), 16)

                with c.loop(DC // 2 - 1, {added: 4 * len(sums), ev("ada_ready0"): 16, ev("ada_ready1"): 16}) as i:
                    two_rows(i * 2, False)
                two_rows(DC - 2, True)
                pool.engine_nop().then_inc(ev("ada_piece"), 1)

            def by_head(t):
                return t[:, :].rearrange("p (m t) -> p m t", t=T)

            def times(t, factor):
                return pool.tensor_tensor(t, t, factor, ALU.mult)

            for d in range(2):
                n = 4 * d
                pool.wait_ge(ev("factors"), n + 1)
                times(qd[d][:, :], gq[:, :])
                times(ki[d][:, :], gk[:, :])
                pool.wait_ge(ev("factors"), n + 2)
                first, second = (gk, gq) if d == 0 else (gq, gk)
                times(by_head(qk[d])[:, :, 0:P], by_head(first)[:, :, 0:P])
                times(by_head(qk[d])[:, :, P:T], by_head(second)[:, :, P:T])
                pool.wait_ge(ev("factors"), n + 3)
                times(kw[d][:, :].rearrange("p (m c t) -> p m c t", m=GH, c=2),
                      gk[:, :].rearrange("p (m c t) -> p m c t", m=GH, c=4)[:, :, d::2, :])
                pool.wait_ge(ev("factors"), n + 4)
                times(qf[d][:, :], gq[:, :]).then_inc(ev("decayed"), 1)

        @block.tensor
        def _(pe):
            c = Counts(pe)
            tile = [0]
            tiles_per = [0]

            def tile_free(n, lag):
                if c.i is not None:
                    pe.wait_ge(tile_read, c.i * tiles_per[0] + (n - lag + 1))
                elif n - lag + 1 > 0:
                    pe.wait_ge(tile_read, n - lag + 1)

            def slot_of_next_unit():
                u = c.n.get("unit", 0)
                pe.wait_ge(lo_ready[u % RING], c.slot_value(u))
                c.n["unit"] = u + 1
                return u % RING

            def units(n, K, hi, lo, sizes=(BLK,), lag=RING, chunks=None, then=None, after=0, final=None):
                blk = 0
                for j in range(n):
                    slot = slot_of_next_unit()
                    for b in range(sizes[j % len(sizes)]):
                        t, k = tile[0] + blk // K, blk % K
                        if k == 0:
                            tile_free(t, lag)
                        dst = ps[t % lag][:, 0:T]
                        w = slice(slot * D + b * P, slot * D + (b + 1) * P)
                        if chunks is not None and j == 0:
                            c.take(chunks)
                        if final is not None and k == K - 1:
                            pe.wait_ge(y_ready, final)
                        pe.matmul(dst, whi[:, w], at(hi, k), start=(k == 0), stop=False)
                        pe.matmul(dst, whi[:, w], at(lo, k), start=False, stop=False)
                        last = pe.matmul(dst, wlo[:, w], at(hi, k), start=False, stop=(k == K - 1))
                        blk += 1
                    c.sig(last, pe_units)
                    if then is not None and j == after:
                        then()
                tile[0] += blk // K

            def looped(times, n, K, hi, lo, sizes=(BLK,), lag=RING, final=None):
                t = tile[0]
                tiles_per[0] = sum(sizes[j % len(sizes)] for j in range(n)) // K
                with c.loop(times, {"unit": n, pe_units: n}):
                    units(n, K, hi, lo, sizes, lag, final=final)
                tile[0] = t + times * tiles_per[0]

            def moving(parts, hi, lo, between={}):
                for j, unit in enumerate(parts):
                    slot = slot_of_next_unit()
                    for half, (k, pair, first, final) in enumerate(unit):
                        w = slice(slot * D + half * 512, slot * D + (half + 1) * 512)
                        for tk in range(2):
                            t = tile[0] + 2 * pair + tk
                            dst = ps[t % RING][:, :]
                            tok = slice(k * T + tk * P, k * T + (tk + 1) * P)
                            if first:
                                tile_free(t, RING)
                            pe.matmul(dst, hi[:, tok], whi[:, w], start=first, stop=False)
                            pe.matmul(dst, lo[:, tok], whi[:, w], start=False, stop=False)
                            last = pe.matmul(dst, hi[:, tok], wlo[:, w], start=False, stop=final)
                    c.sig(last, pe_units)
                    if j in between:
                        between[j]()
                tile[0] += 4

            V_PARTS = [[(2 * j % DC + b, j // 4, 2 * j % DC + b == 0, 2 * j % DC + b == DC - 1) for b in range(2)]
                       for j in range(8)]

            roots_besides = [0]

            def stat_of(pieces, width=T):
                c.n["root_ready"] = c.n.get("stat_ready", 0) + roots_besides[0]
                c.again(root_ready)
                for k, piece in enumerate(pieces):
                    last = pe.matmul(STAT[:, 0:width], ones, piece, start=(k == 0), stop=(k == len(pieces) - 1))
                c.sig(last, stat_ready)

            def stat():
                c.take(ssum_ready, 8)
                stat_of([ssum[:, 0:T]])

            def ada_sums(job, acc, at_col):
                pe.wait_ge(ev("ada_piece"), job + 1)
                for m in range(DC):
                    last = pe.matmul(ps[7][:, at_col * DC + m:at_col * DC + m + 1],
                                     ada_acc[:, acc * D + m * P:acc * D + (m + 1) * P], ones[:, 0:1],
                                     start=True, stop=True)
                last.then_inc(ev("ada_summed"), 1)

            pe.wait_ge(ev("tables"), 32)
            units(3 * DC, DC, xhi, xlo, chunks=x_ready, then=stat, after=1)
            units(DC, DC, yhi, ylo, chunks=y_ready)
            units(4, DC, xhi, xlo, chunks=x_ready, then=stat)
            looped(FC // 2 - 1, 4, DC, xhi, xlo)
            ada_sums(0, 0, 0)
            ada_sums(0, 1, 6)
            c.take(y_ready, FC - 1)
            c.n["y_ready"] += 1
            looped(2, 12, FC, yhi, ylo, (8, 8, 6), final=c.n["y_ready"])
            ada_sums(1, 0, 2)
            units(4, DC, xhi, xlo, chunks=x_ready, then=stat)
            units(4, DC, ohi, olo, chunks=x_ready)
            pe.wait_ge(ev("kv_squares"), 1)
            stat_of([at(ksq, k) for k in range(RK)])
            pe.wait_ge(ev("q_squares"), 1)
            stat_of([at(csq, k) for k in range(RQ)])
            pe.wait_ge(ev("kv_latent"), 1)
            units(2, RK, khi, klo)
            moving([[(k, n, k == 0, k == RK - 1) for n in range(2)] for k in range(RK)], khi, klo)
            pe.wait_ge(ev("q_latent"), 1)
            units(8, RQ, chi, clo)

            def scores(hd):
                if hd >= 2:
                    pe.wait_ge(ev("masked"), hd - 1)
                pe.wait_ge(ev("queries"), hd // 2 + 1)
                for q in range(2):
                    o = ps[hd % 2][:, q * P:q * P + (q + 1) * P]
                    keys = (q + 1) * P
                    pe.matmul(o, qn[:, hd * T + q * P:hd * T + (q + 1) * P], kn[:, hd * T:hd * T + keys],
                              start=True, stop=False)
                    last = pe.matmul(o, qr[:, hd // 2 * T + q * P:hd // 2 * T + (q + 1) * P],
                                     kr[:, hd % 2 * T:hd % 2 * T + keys], start=False, stop=True)
                last.then_inc(ev("scores"), 1)

            def turn(hd):
                pe.wait_ge(ev("weights"), hd + 1)
                if hd >= 2:
                    pe.wait_ge(ev("turned_read"), hd - 1)
                for s in range(3):
                    o = hd % 3 * 3 * P + s * P
                    last = pe.transpose(ps[2 + hd % 2][:, s * P:(s + 1) * P], sm[:, o:o + P], ident)
                last.then_inc(ev("turned"), 1)

            x_before = c.n["x_ready"]

            def values(hd):
                pe.wait_ge(ev("turned_read"), hd + 1)
                if hd >= 2:
                    pe.wait_ge(x_ready, x_before + hd - 1)
                o, p0 = ps[5 + hd % 2], hd % 2 * 3 * P
                pe.matmul(o[:, 0:T], vv[:, hd * P:(hd + 1) * P], pt[:, p0:p0 + T], start=True, stop=False)
                pe.matmul(o[:, P:T], vv[:, D + hd * P:D + (hd + 1) * P], pt[:, p0 + T:p0 + 3 * P], start=False, stop=True)\
                    .then_inc(ev("head_out"), 1)

            ada_sums(2, 1, 3)
            pe.wait_ge(tile_read, tile[0])
            scores(0)
            scores(1)
            for hd in range(HEADS + 1):
                if hd < HEADS:
                    turn(hd)
                    if hd + 2 < HEADS:
                        scores(hd + 2)
                if hd >= 1:
                    values(hd - 1)
            ada_sums(3, 0, 4)
            units(DC, DC, ohi, olo, chunks=x_ready)
            units(4, DC, xhi, xlo, chunks=x_ready, then=stat)
            looped(FC // 2 - 1, 4, DC, xhi, xlo)
            ada_sums(4, 1, 5)
            ada_sums(5, 0, 1)
            c.take(y_ready, FC - 1)
            c.n["y_ready"] += 1
            looped(2, 12, FC, yhi, ylo, (8, 8, 6), final=c.n["y_ready"])
            ada_sums(6, 1, 7)

            def gate_in(n):
                for k in range(DC):
                    last = pe.matmul(ps[7][0:32, 0:T], wa1s[:, k * 32:(k + 1) * 32], at(a32, k),
                                     start=(k == 0), stop=(k == DC - 1))
                last.then_inc(ev("gate_in"), 1)

            def gate_out(n, d):
                i = 2 * n + d
                pe.wait_ge(ev("gate_in_read"), n + 1)
                if i:
                    pe.wait_ge(ev("gate_read"), i)
                for m in range(GH):
                    last = pe.matmul(ps[5 + m // 2][:, m % 2 * T:(m % 2 + 1) * T],
                                     wa2s[:, (d * GH + m) * P:(d * GH + m + 1) * P], t1[:, :], start=True, stop=True)
                last.then_inc(ev("gate_out"), 1)

            c.take(ssum_ready, 16)
            stat_of([ssum[:, :]], 2 * T)
            roots_besides[0] = 1
            pe.wait_ge(ev("tables_late"), 48)
            units(8, DC, xhi, xlo, chunks=x_ready)
            gate_in(0)
            gate_out(0, 0)
            moving(V_PARTS, xhi, xlo)
            stat()
            units(8, DC, xhi, xlo)
            gate_out(0, 1)
            units(4, DC, zhi, zlo, chunks=x_ready)
            gate_in(1)
            moving(V_PARTS, zhi, zlo, {2: lambda: gate_out(1, 0)})
            gate_out(1, 1)
            pe.wait_ge(tile_read, tile[0])
            pe.wait_ge(ev("decayed"), 2)

            def gla_scores(n):
                hd, d = n // 2, n % 2
                dst = ps[n % 4]
                if n >= 4:
                    pe.wait_ge(ev("gla_masked"), n - 3)
                o = hd * T
                for b in range(2):
                    c0 = 2 * P * b
                    pe.matmul(dst[:, c0:c0 + P], ki[d][:, o + b * P:o + (b + 1) * P],
                              qd[d][:, o + b * P:o + (b + 1) * P], start=True, stop=True)
                    keys = kw[d][:, (hd * 2 + b) * CH:(hd * 2 + b + 1) * CH]
                    if d == 0:
                        pe.matmul(dst[0:CH, c0 + CH:c0 + P], keys, qd[d][:, o + b * P + CH:o + (b + 1) * P],
                                  start=True, stop=True)
                    else:
                        pe.matmul(dst[CH:P, c0:c0 + CH], keys, qd[d][:, o + b * P:o + b * P + CH],
                                  start=True, stop=True)
                k0, q0 = (o, o + P) if d == 0 else (o + P, o)
                pe.matmul(dst[:, P:2 * P], qk[d][:, k0:k0 + P], qk[d][:, q0:q0 + P], start=True, stop=True)\
                    .then_inc(ev("gla_scores"), 1)

            def gla_values(hd):
                pe.wait_ge(ev("gla_masked"), 2 * hd + 2)
                if hd >= 3:
                    pe.wait_ge(ev("gla_read"), hd - 2)
                a0, a1 = (2 * hd) % 4 * 3 * P, (2 * hd + 1) % 4 * 3 * P
                for vc in range(2):
                    o = ps[5 + hd % 3][:, vc * T:(vc + 1) * T]
                    v = hd * T + vc * P
                    pe.matmul(o, state[:, v:v + P], at(qf[0], hd), start=True, stop=False)
                    pe.matmul(o, state[:, GH * T + v:GH * T + v + P], at(qf[1], hd), start=False, stop=False)
                    pe.matmul(o, gv[:, v:v + P], att[:, a0:a0 + T], start=False, stop=False)
                    pe.matmul(o, gv[:, D + v:D + v + P], att[:, a1 + P:a1 + 3 * P], start=False, stop=False)
                    pe.matmul(o[:, P:T], gv[:, D + v:D + v + P], att[:, a0 + T:a0 + 3 * P], start=False, stop=False)
                    last = pe.matmul(o[:, 0:P], gv[:, v:v + P], att[:, a1:a1 + P], start=False, stop=True)
                last.then_inc(ev("gla_out"), 1)

            for n in range(4):
                gla_scores(n)
            for d in range(2):
                pe.wait_ge(ev("ctx_decayed"), d + 1)
                pe.wait_ge(ev("gla_masked"), 4)
                for tk in range(2):
                    if 2 * d + tk:
                        pe.wait_ge(ev("ctx_turned_read"), 2 * d + tk)
                    for m in range(GH):
                        o = (d * GH + m) * T + tk * P
                        last = pe.transpose(ps[7][:, m * P:(m + 1) * P], a32[:, o:o + P], ident)
                    last.then_inc(ev("ctx_turned"), 1)
                pe.wait_ge(ev("ctx_turned_read"), 2 * d + 2)
                for m in range(GH):
                    dst = ps[2 * d + m // 2][:, m % 2 * T:(m % 2 + 1) * T]
                    for tk in range(2):
                        last = pe.matmul(dst, kt[:, (tk * GH + m) * P:(tk * GH + m + 1) * P],
                                         cval[:, tk * D + m * T:tk * D + (m + 1) * T], start=(tk == 0), stop=(tk == 1))
                last.then_inc(ev("state_out"), 1)

            pe.wait_ge(ev("state_read"), 2)
            for hd in range(GH + 1):
                if hd < GH:
                    gla_values(hd)
                if hd >= 1:
                    pe.wait_ge(ev("gla_squares"), hd)
                    stat_of([osq[:, 0:T], osq[:, T:2 * T]])
                if hd + 2 < GH:
                    gla_scores(2 * hd + 4)
                    gla_scores(2 * hd + 5)
            units(DC, DC, zhi, zlo, chunks=y_ready)
            stat()
            units(4, DC, xhi, xlo, chunks=x_ready)
            looped(MC // 4 - 1, 4, DC, xhi, xlo)
            c.take(y_ready, MC - 1)
            c.n["y_ready"] += 1
            looped(DC // 2, 8, MC, mhi, mlo, lag=2, final=c.n["y_ready"])
            stat()

        @block.scalar
        def _(act):
            c = Counts(act)

            def settled():
                act.wait_ge(ev("tables"), 32)

            def hi(n=1):
                for _ in range(n):
                    u = c.n.get("hi_ready", 0)
                    if u >= UNITS:
                        return
                    s = u % RING
                    landed = 16 * (u // RING + 1)
                    if c.i is not None:
                        landed = c.i * (4 * c.per["hi_ready"]) + landed
                    act.wait_ge(raw_ready[s], landed)
                    if u >= RING:
                        act.wait_ge(pe_units, c.value(hi_ready, 1 - RING))
                    c.sig(act.activation(whi[:, s * D:(s + 1) * D], raw[:, s * D:(s + 1) * D], ACT.Copy), hi_ready)

            def square(src, k, slot, scale=1.0):
                if c.n.get("sq_ready", 0) >= 2:
                    added = c.value(sq_ready, -1)
                    if c.i is not None:
                        added = act.to_reg(added)
                        settled()
                    act.wait_ge(ssum_ready, added)
                c.sig(act.activation(at(sq, slot % 2), at(src, k), ACT.Square, scale=scale), sq_ready)

            def sqrt_stat(n):
                c.n["rstd_ready"] = c.n.get("root_ready", 0)
                c.again(rstd_ready)
                c.take(stat_ready)
                c.sig(act.activation(root[:, :], STAT[:, 0:T], ACT.Sqrt, scale=1.0 / n, bias=EPS), root_ready)

            def ffn_up(conv):
                base = VEC[conv][0]

                def steps(i, first):
                    for j in range(4):
                        if j != 0:
                            hi()
                        if j % 2 == 0 and not (first and j == 0):
                            c.take(conv_ready)
                            c.sig(act.activation(at(sil, 1 - j // 2), at(cv, (j + 2) % 4), ACT.Silu), sil_ready)
                            c.n["conv_ready"] += 1
                        if j == 0:
                            hi()
                        if j % 2 == 1 and not (first and j == 1):
                            settled()
                            c.take(y_f32)
                            c.sig(act.activation(at(yhi, i * 2 + (j // 2 - 1)), at(prod, 1 - j // 2), ACT.Copy),
                                  yhi_ready)
                        settled()
                        c.take(tile_read)
                        c.sig(act.activation(at(cv, j), U[:, j * (T + 2) + 2:(j + 1) * (T + 2)], ACT.Copy,
                                             scale=vt_col(i * 12 + (base + 3 * j + 2))), tap_ready)

                steps(0, True)
                with c.loop(FC // 2 - 1, {hi_ready: 4, tile_read: 4, tap_ready: 4, conv_ready: 4, sil_ready: 2,
                                          y_f32: 2, yhi_ready: 2}) as i:
                    steps(i + 1, False)
                c.take(conv_ready)
                c.sig(act.activation(at(sil, 1), at(cv, 2), ACT.Silu), sil_ready)
                c.n["conv_ready"] += 1
                c.take(y_f32)
                c.sig(act.activation(at(yhi, FC - 1), at(prod, 1), ACT.Copy), yhi_ready)

            def resid(units_per, gain, gained=None):
                per = {hi_ready: 4 * units_per, tile_read: 4, sq_ready: 8 if gained else 4}
                if gain:
                    per[xhi_ready] = 4
                with c.loop(2, per) as i:
                    for m in range(4):
                        hi(units_per)
                        settled()
                        c.take(tile_read)
                        if gain:
                            c.sig(act.activation(at(xhi, i * 4 + m), at(h, i * 4 + m), ACT.Copy,
                                                 scale=vt[:, bass.ds(i * 4 + (VEC[gain][0] + m), 1)]), xhi_ready)
                        square(h, i * 4 + m, 0 if gained else m)
                        if gained:
                            square(h, i * 4 + m, 1, vt_col(i * 4 + (VEC[gained][0] + m)))

            act.wait_ge(ev("tables"), 32)
            act.activation(sc[:, :], vt[:, VEC["c"][0]:VEC["c"][0] + 16], ACT.Silu).then_inc(ev("sc_ready"), 1)
            act.wait_ge(ev("x_loaded"), 16)
            for k in range(DC):
                c.sig(act.activation(at(xhi, k), at(h, k), ACT.Copy, scale=col("g_mix0", k)), xhi_ready)
                if k == 3:
                    hi()
            hi(2)
            for k in range(DC):
                square(h, k, k)
            sqrt_stat(D)
            with c.loop(2, {hi_ready: 12, u_ready: 4, tap_ready: 4, y_f32: 4, yhi_ready: 4}) as i:
                def split_hi(j):
                    settled()
                    c.take(y_f32)
                    c.sig(act.activation(at(yhi, i * 4 + j), at(prod, j % 2), ACT.Copy), yhi_ready)

                for j in range(4):
                    hi()
                    if j:
                        split_hi(j - 1)
                    hi()
                    settled()
                    c.take(u_ready)
                    c.sig(act.activation(at(cv, j), U[:, j * (T + 2) + 2:(j + 1) * (T + 2)], ACT.Copy,
                                         scale=vt_col(i * 12 + (VEC["conv_mix"][0] + 3 * j + 2))), tap_ready)
                    hi()
                split_hi(3)
            c.n["tile_read"] = 3 * DC
            resid(1, "g_ffn0")
            sqrt_stat(D)
            ffn_up("conv0")
            resid(3, "g_kvin")
            sqrt_stat(D)
            for u in range(4):
                hi()
                for k in range(2 * u, 2 * u + 2):
                    c.sig(act.activation(at(ohi, k), at(h, k), ACT.Copy, scale=col("g_mix1", k)), xhi_ready)
            c.take(tile_read, 2)
            act.activation(ksq[:, :], kf[:, :], ACT.Square).then_inc(ev("kv_squares"), 1)
            hi(4)
            c.take(tile_read, 6)
            act.activation(csq[:, :], cf[:, :], ACT.Square).then_inc(ev("q_squares"), 1)
            sqrt_stat(RK * P)
            sqrt_stat(RQ * P)
            act.wait_ge(ev("kv_normed"), 1)
            act.activation(khi[:, :], kf[:, :], ACT.Copy).then_inc(ev("khi_ready"), 1)
            hi()
            act.wait_ge(ev("q_normed"), 1)
            act.activation(chi[:, :], cf[:, :], ACT.Copy).then_inc(ev("chi_ready"), 1)
            hi(11)
            c.n["tile_read"] += 8 + 4 + 16
            for hd in range(HEADS + 3):
                if hd >= 3:
                    g = hd - 3
                    act.wait_ge(ev("head_out"), g + 1)
                    c.sig(act.activation(at(ohi, g), ps[5 + g % 2][:, 0:T], ACT.Copy), xhi_ready)
                if hd < HEADS:
                    act.wait_ge(ev("negmax"), hd + 1)
                    m0 = hd % 3 * 8
                    for q in range(2):
                        s0 = hd % 3 * 3 * P + q * P
                        s = sm[:, s0:s0 + (q + 1) * P]
                        last = act.activation(s, s, ACT.Exp, bias=mx[:, m0 + 2 + q:m0 + 3 + q],
                                              accum_out=mx[:, m0 + 4 + q:m0 + 5 + q])
                    last.then_inc(ev("exps"), 1)
                if 1 <= hd <= HEADS:
                    g = hd - 1
                    act.wait_ge(ev("turned"), g + 1)
                    if g >= 2:
                        act.wait_ge(ev("head_out"), g - 1)
                    act.activation(pt[:, g % 2 * 3 * P:(g % 2 + 1) * 3 * P], ps[2 + g % 2][:, 0:3 * P], ACT.Copy)\
                        .then_inc(ev("turned_read"), 1)
            resid(1, "g_ffn1")
            sqrt_stat(D)
            ffn_up("conv1")
            resid(3, None, "g_fin1")

            def modulated(dst, beside=False):
                for k in range(DC):
                    if beside and k % 2:
                        hi()
                    c.take(a_ready)
                    c.sig(act.activation(at(dst, k), at(a32, k), ACT.Copy), xhi_ready)

            def log_gate(i):
                if i in (1, 2):
                    act.wait_ge(ev("factors"), 4 * i)
                act.wait_ge(ev("gate_out"), i + 1)
                for m in range(GH):
                    last = act.activation(at(za, m), ps[5 + m // 2][:, m % 2 * T:(m % 2 + 1) * T], ACT.Abs,
                                          bias=col("b_gate", i % 2 * GH + m))
                last.then_inc(ev("gate_abs"), 1)
                act.wait_ge(ev("gate_abs"), i + 1)
                act.activation(za[:, :], za[:, :], ACT.Exp, scale=-1.0).then_inc(ev("gate_exp"), 1)
                act.wait_ge(ev("gate_exp"), i + 1)
                act.activation(za[:, :], za[:, :], ACT.Ln, bias=1.0).then_inc(ev("gate_ln"), 1)

            def by_head(t, w=T):
                return t[:, :].rearrange("p (m t) -> p m t", t=w)

            def decays(d, part):
                s = INV_TAU if d == 0 else -INV_TAU
                act.wait_ge(ev("expo"), 4 * d + part + 1)
                if part == 0:
                    act.activation(qd[d][:, :], za[:, :], ACT.Exp, scale=s)
                    last = act.activation(ki[d][:, :], za[:, :], ACT.Exp, scale=-s)
                elif part == 1:
                    act.activation(by_head(qk[d])[:, :, 0:P], by_head(zm)[:, :, 0:P], ACT.Exp, scale=-INV_TAU)
                    last = act.activation(by_head(qk[d])[:, :, P:T], by_head(zm)[:, :, P:T], ACT.Exp, scale=INV_TAU)
                elif part == 2:
                    last = act.activation(kw[d][:, :], za[:, 0:GH * 2 * CH], ACT.Exp, scale=-s)
                else:
                    last = act.activation(qf[d][:, :], zm[:, :], ACT.Exp, scale=s)
                last.then_inc(ev("factors"), 1)

            sqrt_stat(D)
            act.wait_ge(ev("var_ready"), 1)
            c.sig(act.activation(root[:, :], at(sq, 0), ACT.Sqrt, scale=1.0 / D, bias=EPS), root_ready)
            modulated(xhi)
            hi(8)
            c.take(tile_read, 8)
            act.wait_ge(ev("gate_in"), 1)
            act.dma_start(a32[:, :], ctxT).then_inc(ev("ctx_loaded"), 16)
            hi(2)
            log_gate(0)
            hi(2)
            act.wait_ge(ev("ctx_loaded"), 16)
            for k in range(DC):
                if k % 2 == 0:
                    hi()
                square(a32, k, k)
            hi()
            sqrt_stat(D)
            modulated(zhi, True)
            c.n["tile_read"] += 4
            for m in range(4, DC):
                if m >= 5:
                    hi()
                decays(0, m - 4)
            hi(2)
            log_gate(1)
            hi(2)
            for part in range(4):
                hi()
                decays(1, part)
            hi()
            log_gate(2)

            def ctx_factors(d):
                act.wait_ge(ev("expo"), 9 + d)
                act.activation(a32[:, d * GH * T:(d + 1) * GH * T], za[:, :], ACT.Exp,
                               scale=-INV_TAU if d == 0 else INV_TAU).then_inc(ev("factors"), 1)

            ctx_factors(0)
            act.wait_ge(ev("factors"), 9)
            log_gate(3)
            ctx_factors(1)
            hi(3)
            c.take(tile_read, 16)
            act.activation(rsil[:, :], rsil[:, :], ACT.Silu).then_inc(ev("rsil_ready"), 1)
            for hd in range(GH):
                act.wait_ge(ev("gla_out"), hd + 1)
                act.activation(osq[:, :], ps[5 + hd % 3][:, :], ACT.Square).then_inc(ev("gla_squares"), 1)
                sqrt_stat(2 * P)
                for vc in range(2):
                    c.take(y_f32)
                    c.sig(act.activation(at(zhi, 2 * hd + vc), at(rsil, 2 * hd + vc), ACT.Copy), yhi_ready)
            resid(1, None)
            sqrt_stat(D)
            modulated(xhi)
            c.n["pe_units"] = UNITS - 2 * MC
            with c.loop(MC // 4, {hi_ready: 4, pe_units: 4, tile_read: 4, y_f32: 4, yhi_ready: 4}) as i:
                def inner_hi(j):
                    settled()
                    c.take(y_f32)
                    c.sig(act.activation(at(mhi, i * 4 + j), at(ms, j), ACT.Copy), yhi_ready)

                for j in range(4):
                    hi()
                    c.take(pe_units)
                    c.sig(act.activation(at(mr, j), ps[j][:, 0:T], ACT.Relu), tile_read)
                    if j:
                        inner_hi(j - 1)
                inner_hi(3)

            def mlp_down(first):
                for m in range(2):
                    hi(4)
                    c.take(tile_read)
                    square(h, first + m, m)

            with c.loop(DC // 2 - 1, {hi_ready: 8, tile_read: 2, sq_ready: 2}) as i:
                mlp_down(i * 2)
            mlp_down(DC - 2)
            sqrt_stat(D)

        @block.vector
        def _(dve):
            c = Counts(dve)
            tile = [0]

            def lo(n=1):
                for _ in range(n):
                    u = c.n.get("unit", 0)
                    if u >= UNITS:
                        return
                    w = slice(u % RING * D, (u % RING + 1) * D)
                    c.take(hi_ready)
                    dve.tensor_tensor(wlo[:, w], raw[:, w], whi[:, w], ALU.subtract).then_inc(lo_ready[u % RING], 1)
                    c.n["unit"] = u + 1

            def link(ins):
                c.sig(ins, seq_dve)
                c.again(seq_dve)

            def result(n_units, width=T):
                if n_units:
                    c.take(pe_units, n_units)
                tile[0] += 1
                return ps[(tile[0] - 1) % RING][:, 0:width]

            def add_square(k, which=0):
                c.take(sq_ready)
                c.again(ssum_ready)
                c.sig(dve.tensor_tensor(at(ssum, which), at(ssum, which), at(sq, k % 2), ALU.add), ssum_ready)

            def split_lo(k, gain):
                c.take(xhi_ready)
                c.sig(dve.scalar_tensor_tensor(out=at(xlo, k), in0=at(h, k), scalar=gain, in1=at(xhi, k),
                                               op0=ALU.mult, op1=ALU.subtract), x_ready)

            def reciprocal_root(dst):
                c.take(root_ready)
                c.sig(dve.reciprocal(dst[:, :], root[:, :]), rstd_ready)
                c.again(rstd_ready)

            def clear_sum():
                link(dve.memset(ssum[:, :], 0.0))

            def tap_one(j, w1):
                c.take(tap_ready)
                o = j * (T + 2)
                c.sig(dve.scalar_tensor_tensor(out=at(cv, j), in0=U[:, o + 1:o + T + 1], scalar=w1, in1=at(cv, j),
                                               op0=ALU.mult, op1=ALU.add), seq_dve)

            def tap_zero(j, w0):
                o = j * (T + 2)
                return dve.scalar_tensor_tensor(out=at(cv, j), in0=U[:, o:o + T], scalar=w0, in1=at(cv, j),
                                                op0=ALU.mult, op1=ALU.add)

            def ffn_up(conv, own):
                base = VEC[conv][0]

                def product(f):
                    c.take(sil_ready)
                    c.again(conv_ready)
                    c.sig(dve.tensor_tensor(at(prod, f), at(sil, f), at(cv, 2 * f + 1), ALU.mult), y_f32)

                def product_lo(k, f):
                    c.take(yhi_ready)
                    c.sig(dve.tensor_tensor(at(ylo, k), at(prod, f), at(yhi, k), ALU.subtract), y_ready)

                def steps(i, first, alone):
                    for j in range(4):
                        older = not (first and j == 0)
                        if older:
                            w = i * 12 + (base + 3 * j - 3)
                            tap_one((j - 1) % 4, vt_col(w + 1))
                        c.sig(dve.tensor_tensor(U[:, j * (T + 2) + 2:(j + 1) * (T + 2)], result(1), rstd[:, :],
                                                ALU.mult), tile_read)
                        if older:
                            c.again(seq_dve)
                            c.sig(tap_zero((j - 1) % 4, vt_col(w)), conv_ready)
                            if j % 2 == 0:
                                product(1 - j // 2)
                            elif j > 1 or not first:
                                product_lo(i * 2 + (j // 2 - 1), 1 - j // 2)
                        if j or alone:
                            lo()
                        else:
                            c.n["hi_ready"] += 1
                            c.n["unit"] += 1

                per = {hi_ready: 4, "unit": 4, pe_units: 4, tile_read: 4, tap_ready: 4, conv_ready: 4, sil_ready: 2,
                       y_f32: 2, yhi_ready: 2, y_ready: 2, seq_dve: 4}
                steps(0, True, own > 0)
                if own:
                    with c.loop(own - 1, per) as i:
                        steps(i + 1, False, True)
                start = max(own, 1)
                with c.loop(FC // 2 - start, per) as i:
                    steps(i + start, False, False)
                w = base + 3 * (2 * FC - 1)
                tap_one(3, vt_col(w + 1))
                c.again(seq_dve)
                c.sig(tap_zero(3, vt_col(w)), conv_ready)
                product(1)
                product_lo(FC - 1, 1)

            def resid(units_per, gain, gate=None, gained=False):
                clear_sum()
                n = 4 * units_per
                squares = 8 if gained else 4
                per = {hi_ready: n, "unit": n, pe_units: n, tile_read: 4, sq_ready: squares, ssum_ready: squares}
                if gain:
                    per |= {xhi_ready: 4, x_ready: 4}
                with c.loop(2, per) as i:
                    def finish(m):
                        if gain:
                            split_lo(i * 4 + m, vt_col(i * 4 + (VEC[gain][0] + m)))
                            add_square(m)
                        elif gained:
                            add_square(0)
                            add_square(1, 1)
                        else:
                            add_square(m)

                    for m in range(4):
                        if units_per > 1:
                            lo(units_per)
                        r, hm = result(units_per), at(h, i * 4 + m)
                        if gate is None:
                            ins = dve.tensor_tensor(hm, r, hm, ALU.add)
                        else:
                            ins = dve.scalar_tensor_tensor(out=hm, in0=r, scalar=mod[:, bass.ds(i * 4 + (gate + m), 1)],
                                                           in1=hm, op0=ALU.mult, op1=ALU.add)
                        c.sig(ins, tile_read)
                        if m:
                            finish(m - 1)
                        if units_per == 1:
                            lo()
                    finish(3)

            dve.memset(U[:, :], 0.0).then_inc(ev("pads"), 1)
            clear_sum()
            dve.wait_ge(ev("tables"), 32)
            dve.wait_ge(ev("x_loaded"), 16)
            for k in range(DC):
                split_lo(k, col("g_mix0", k))
                if k == 3:
                    lo()
            lo(2)
            for k in range(DC):
                add_square(k)
            reciprocal_root(rstd)
            dve.wait_ge(ev("pads"), 1)
            with c.loop(2, {hi_ready: 12, "unit": 12, pe_units: 12, tile_read: 12, u_ready: 4, tap_ready: 4,
                            y_f32: 4, yhi_ready: 4, y_ready: 4, seq_dve: 8}) as i:
                def split_lo_of(j):
                    c.take(yhi_ready)
                    c.sig(dve.tensor_tensor(at(ylo, i * 4 + j), at(prod, j % 2), at(yhi, i * 4 + j), ALU.subtract),
                          y_ready)

                for j in range(4):
                    c.sig(dve.tensor_tensor(at(sil, 0), result(1), rstd[:, :], ALU.mult), tile_read)
                    lo()
                    if j:
                        split_lo_of(j - 1)
                    c.sig(dve.tensor_tensor(at(sil, 1), result(1), rstd[:, :], ALU.mult), tile_read)
                    c.again(tile_read)
                    c.sig(dve.tensor_tensor(U[:, j * (T + 2) + 2:(j + 1) * (T + 2)], at(sil, 0), at(sil, 1), ALU.mult),
                          u_ready)
                    lo()
                    w = i * 12 + (VEC["conv_mix"][0] + 3 * j)
                    tap_one(j, vt_col(w + 1))
                    c.sig(dve.tensor_tensor(at(prod, j % 2), result(1), rstd[:, :], ALU.mult), tile_read)
                    c.again(seq_dve)
                    link(tap_zero(j, vt_col(w)))
                    c.again(tile_read)
                    c.sig(dve.tensor_tensor(at(prod, j % 2), at(prod, j % 2), at(cv, j), ALU.mult), y_f32)
                    lo()
                split_lo_of(3)
            resid(1, "g_ffn0")
            reciprocal_root(rstd)

            ffn_up("conv0", 0)
            resid(3, "g_kvin")
            reciprocal_root(rstd)
            for u in range(4):
                lo()
                for k in range(2 * u, 2 * u + 2):
                    c.take(xhi_ready)
                    c.sig(dve.scalar_tensor_tensor(out=at(olo, k), in0=at(h, k), scalar=col("g_mix1", k),
                                                   in1=at(ohi, k), op0=ALU.mult, op1=ALU.subtract), x_ready)
                dst = at(kf, u) if u < RK else at(rt, u - RK)
                c.sig(dve.tensor_tensor(dst, result(1), rstd[:, :], ALU.mult), tile_read)
            dve.wait_ge(ev("tables_late"), 48)
            c.again(tile_read)
            for half, names in enumerate((("cos_a", "sin_a"), ("cos_b", "sin_b"))):
                dve.tensor_tensor(at(rt, 2), at(rt, 0), rot_of(names[0]), ALU.mult)
                link(dve.tensor_tensor(at(rt, 3), at(rt, 1), rot_of(names[1]), ALU.mult))
                link(dve.tensor_tensor(at(kr, half), at(rt, 2), at(rt, 3), ALU.add))
            for j in range(RQ):
                lo()
                c.sig(dve.tensor_tensor(at(cf, j), result(1), rstd[:, :], ALU.mult), tile_read)
            reciprocal_root(rk)
            for k in range(RK):
                last = dve.scalar_tensor_tensor(out=at(kf, k), in0=at(kf, k), scalar=col("g_kv", k), in1=rk[:, :],
                                                op0=ALU.mult, op1=ALU.mult)
            last.then_inc(ev("kv_normed"), 1)
            dve.wait_ge(ev("khi_ready"), 1)
            dve.tensor_tensor(klo[:, :], kf[:, :], khi[:, :], ALU.subtract).then_inc(ev("kv_latent"), 1)
            def keys(u):
                for m in range(4):
                    c.sig(dve.tensor_copy(at(kn, 4 * u + m), result(m == 0)), tile_read)
                lo()

            reciprocal_root(rq)
            for k in range(RQ):
                last = dve.scalar_tensor_tensor(out=at(cf, k), in0=at(cf, k), scalar=col("g_q", k), in1=rq[:, :],
                                                op0=ALU.mult, op1=ALU.mult)
            last.then_inc(ev("q_normed"), 1)
            keys(0)
            keys(1)
            dve.wait_ge(ev("chi_ready"), 1)
            dve.tensor_tensor(clo[:, :], cf[:, :], chi[:, :], ALU.subtract).then_inc(ev("q_latent"), 1)
            lo(2)
            for n in range(2):
                for tk in range(2):
                    c.sig(dve.tensor_copy(vv[:, tk * D + n * 512:tk * D + (n + 1) * 512],
                                          result(2 if n + tk == 0 else 0, 512)), tile_read)
            for u in range(4):
                lo()
                for m in range(2):
                    c.sig(dve.tensor_scalar(at(qn, 2 * u + m), result(m == 0), QK_SCALE, None, ALU.mult), tile_read)
            for u in range(4):
                lo()
                for m in range(2):
                    c.sig(dve.tensor_scalar(at(rt, m), result(m == 0), QK_SCALE, None, ALU.mult), tile_read)
                c.again(tile_read)
                dve.tensor_tensor(at(rt, 2), at(rt, 0), rot_of("cos_q"), ALU.mult)
                link(dve.tensor_tensor(at(rt, 3), at(rt, 1), rot_of("sin_q"), ALU.mult))
                dve.tensor_tensor(at(qr, u), at(rt, 2), at(rt, 3), ALU.add).then_inc(ev("queries"), 1)
                dve.wait_ge(ev("queries"), u + 1)
            for hd in range(HEADS + 3):
                if 1 <= hd <= HEADS:
                    g = hd - 1
                    s0, m0 = g % 3 * 3 * P, g % 3 * 8
                    dve.wait_ge(ev("exps"), g + 1)
                    link(dve.reciprocal(mx[:, m0 + 6:m0 + 8], mx[:, m0 + 4:m0 + 6]))
                    dve.tensor_scalar(sm[:, s0:s0 + P], sm[:, s0:s0 + P], mx[:, m0 + 6:m0 + 7], None, ALU.mult)
                    dve.tensor_scalar(sm[:, s0 + P:s0 + 3 * P], sm[:, s0 + P:s0 + 3 * P], mx[:, m0 + 7:m0 + 8], None,
                                      ALU.mult).then_inc(ev("weights"), 1)
                if hd < HEADS:
                    s0, m0 = hd % 3 * 3 * P, hd % 3 * 8
                    dve.wait_ge(ev("scores"), hd + 1)
                    if hd >= 3:
                        dve.wait_ge(ev("turned"), hd - 2)
                    dve.tensor_tensor(sm[:, s0:s0 + 3 * P], ps[hd % 2][:, 0:3 * P], rot_of("mask_s"), ALU.add)\
                        .then_inc(ev("masked"), 1)
                if hd >= 3:
                    g = hd - 3
                    c.take(xhi_ready)
                    c.sig(dve.tensor_tensor(at(olo, g), ps[5 + g % 2][:, 0:T], at(ohi, g), ALU.subtract), x_ready)
                if hd < HEADS:
                    dve.wait_ge(ev("masked"), hd + 1)
                    dve.tensor_reduce(mx[:, m0:m0 + 1], sm[:, s0:s0 + P], AX.X, ALU.max)
                    link(dve.tensor_reduce(mx[:, m0 + 1:m0 + 2], sm[:, s0 + P:s0 + 3 * P], AX.X, ALU.max))
                    dve.tensor_scalar(mx[:, m0 + 2:m0 + 4], mx[:, m0:m0 + 2], -1.0, None, ALU.mult)\
                        .then_inc(ev("negmax"), 1)
            resid(1, "g_ffn1")
            reciprocal_root(rstd)
            pads = U[:, :].rearrange("p (j t) -> p j t", t=T + 2)[:, :, 0:2]
            link(dve.memset(pads, 0.0))
            ffn_up("conv1", OWN_GROUPS)
            resid(3, None, gained=True)

            def modulated(src, g0, s0, lo_dst, beside=False):
                for k in range(DC + 2):
                    if k < DC:
                        c.sig(dve.scalar_tensor_tensor(out=at(a32, k), in0=at(src, k), scalar=gmod[:, g0 + k:g0 + k + 1],
                                                       in1=rstd[:, :], op0=ALU.mult, op1=ALU.mult), seq_dve)
                    if 1 <= k <= DC:
                        c.again(seq_dve, 1 if k < DC else 0)
                        c.sig(dve.tensor_scalar(at(a32, k - 1), at(a32, k - 1), mod[:, s0 + k - 1:s0 + k], None, ALU.add),
                              a_ready)
                    if k >= 2:
                        c.take(xhi_ready)
                        c.sig(dve.tensor_tensor(at(lo_dst, k - 2), at(a32, k - 2), at(xhi if lo_dst is xlo else zhi, k - 2),
                                                ALU.subtract), x_ready)
                    if beside and k % 2 == 0 and k >= 2:
                        if k >= 4:
                            c.sig(dve.tensor_copy(at(rsil, k // 2 - 2), result(1)), tile_read)
                        lo()

            def by_head(t, w=T):
                return t[:, :].rearrange("p (m t) -> p m t", t=w)

            def border(first, step, n, width):
                v = by_head(pb, T + 1)[:, :, first:first + step * (n - 1) + 1:step]
                return v.unsqueeze(3).to_broadcast([P, GH, n, width])

            def one_border(first):
                return by_head(pb, T + 1)[:, :, first:first + 1].to_broadcast([P, GH, T])

            def log_decay(i, bank0=5):
                dve.wait_ge(ev("gate_abs"), i + 1)
                if i in (1, 2):
                    dve.wait_ge(ev("factors"), 4 * i)
                for m in range(GH):
                    last = dve.tensor_scalar(at(zm, m), ps[bank0 + m // 2][:, m % 2 * T:(m % 2 + 1) * T],
                                             col("b_gate", i % 2 * GH + m), 0.0, ALU.add, ALU.min)
                last.then_inc(ev("gate_read"), 1)
                dve.wait_ge(ev("gate_read"), i + 1)
                dve.wait_ge(ev("gate_ln"), i + 1)
                link(dve.tensor_tensor(zm[:, :], zm[:, :], za[:, :], ALU.subtract))
                for m in range(GH):
                    last = dve.tensor_tensor_scan(out=pb[:, m * (T + 1) + 1:(m + 1) * (T + 1)], data0=one_t[:, :],
                                                  data1=at(zm, m), initial=0.0, op0=ALU.mult, op1=ALU.add)
                link(last)

            def chunks(t, n):
                return t.rearrange("p (m c t) -> p m c t", m=GH, c=n)

            def decays(d, part):
                sums = by_head(pb, T + 1)[:, :, 1 - d:T + 1 - d]
                by_chunk = sums.rearrange("p m (c t) -> p m c t", t=CH)
                if part == 0:
                    ins = dve.tensor_tensor(chunks(za[:, :], 4), by_chunk, border(CH * d, CH, 4, CH), ALU.subtract)
                elif part == 1:
                    ins = dve.tensor_tensor(by_head(zm), sums, one_border(P), ALU.subtract)
                elif part == 2:
                    dve.wait_ge(ev("factors"), 4 * d + 1)
                    ins = dve.tensor_tensor(chunks(za[:, 0:GH * 2 * CH], 2), by_chunk[:, :, d::2, :],
                                            border(CH, P, 2, CH), ALU.subtract)
                else:
                    dve.wait_ge(ev("factors"), 4 * d + 2)
                    ins = (dve.tensor_copy(by_head(zm), sums) if d == 0 else
                           dve.tensor_tensor(by_head(zm), sums, one_border(T), ALU.subtract))
                ins.then_inc(ev("expo"), 1)

            dve.wait_ge(ev("ada_summed"), 8)
            b_ada = VEC["b_ada"][0]
            dve.tensor_tensor(mod[:, 0:48], ps[7][:, 0:48], vt[:, b_ada:b_ada + 48], ALU.add)
            link(dve.tensor_tensor(mod[:, 48:64], ps[7][:, 48:64], vt[:, b_ada:b_ada + 16], ALU.add))
            for n, (scale, gain) in enumerate(((8, "g_n1"), (32, "g_n2"), (56, "g_n1"))):
                link(dve.scalar_tensor_tensor(out=gmod[:, n * DC:(n + 1) * DC], in0=mod[:, scale:scale + DC], scalar=1.0,
                                              in1=vt[:, VEC[gain][0]:VEC[gain][0] + DC], op0=ALU.add, op1=ALU.mult))
            g = VEC["g_fin1"][0]
            link(dve.tensor_tensor(gmod[:, 0:DC], gmod[:, 0:DC], vt[:, g:g + DC], ALU.mult))
            first_rstd = sq[:, T:2 * T]
            reciprocal_root(first_rstd)
            link(dve.tensor_tensor(at(sq, 0), STAT[:, T:2 * T], first_rstd, ALU.mult))
            dve.tensor_tensor(at(sq, 0), at(sq, 0), first_rstd, ALU.mult).then_inc(ev("var_ready"), 1)
            reciprocal_root(rstd)
            link(dve.tensor_tensor(rstd[:, :], rstd[:, :], first_rstd, ALU.mult))
            modulated(h, 0, 0, xlo)
            dve.memset(one_t[:, :], 1.0)
            link(dve.memset(pb[:, :], 0.0))
            def final_norm(k):
                ins = dve.scalar_tensor_tensor(out=at(h, k), in0=at(h, k), scalar=col("g_fin1", k), in1=first_rstd,
                                               op0=ALU.mult, op1=ALU.mult)
                if k == DC - 1:
                    link(ins)

            for m in range(GH):
                lo()
                c.sig(dve.tensor_scalar(at(gq, m), result(1), GLA_SCALE, None, ALU.mult), tile_read)
                final_norm(m)
            for m in range(GH):
                lo()
                c.sig(dve.tensor_copy(at(gk, m), result(1)), tile_read)
                final_norm(GH + m)
            dve.wait_ge(ev("gate_in"), 1)
            dve.tensor_copy(t1[:, :], ps[7][0:32, 0:T]).then_inc(ev("gate_in_read"), 1)
            clear_sum()
            lo(2)
            log_decay(0)
            lo(2)
            for k in range(DC):
                if k % 2 == 0:
                    lo()
                add_square(k)
            for n in range(2):
                for tk in range(2):
                    c.sig(dve.tensor_copy(gv[:, tk * D + n * 512:tk * D + (n + 1) * 512],
                                          result(8 if n + tk == 0 else 0, 512)), tile_read)
            lo()
            reciprocal_root(rstd)
            modulated(a32, 2 * DC, 6 * DC, zlo, True)
            for m in range(3, DC):
                c.sig(dve.tensor_copy(at(rsil, m), result(1)), tile_read)
                if m >= 5:
                    lo()
                if m >= 4:
                    decays(0, m - 4)
            for m in range(GH):
                c.sig(dve.tensor_copy(at(ck, m), result(1)), tile_read)
                lo()
                if m == 1:
                    log_decay(1)
            dve.wait_ge(ev("gate_in"), 2)
            dve.wait_ge(ev("gate_out"), 2)
            dve.tensor_copy(t1[:, :], ps[7][0:32, 0:T]).then_inc(ev("gate_in_read"), 1)
            for part in range(4):
                lo()
                decays(1, part)
            lo()

            def ctx_exponents(d):
                log_decay(2 + d)
                sums = by_head(pb, T + 1)[:, :, 1 - d:T + 1 - d]
                dve.tensor_tensor(by_head(za), sums, one_border(T if d == 0 else 0),
                                  ALU.subtract).then_inc(ev("expo"), 1)

            def ctx_keys(d):
                w = slice(d * GH * T, (d + 1) * GH * T)
                dve.wait_ge(ev("factors"), 9 + d)
                dve.tensor_tensor(a32[:, w], a32[:, w], ck[:, :], ALU.mult).then_inc(ev("ctx_decayed"), 1)

            def ctx_state(d):
                w = slice(d * GH * T, (d + 1) * GH * T)
                for tk in range(2):
                    dve.wait_ge(ev("ctx_turned"), 2 * d + tk + 1)
                    if d:
                        dve.wait_ge(ev("state_out"), 1)
                    dve.tensor_copy(kt[:, tk * GH * P:(tk + 1) * GH * P], ps[7][:, :]).then_inc(ev("ctx_turned_read"), 1)
                dve.wait_ge(ev("state_out"), d + 1)
                dve.tensor_copy(state[:, w.start:w.start + 512], ps[2 * d][:, :])
                dve.tensor_copy(state[:, w.start + 512:w.stop], ps[2 * d + 1][:, :]).then_inc(ev("state_read"), 1)

            ctx_exponents(0)
            for n in range(2):
                for tk in range(2):
                    c.sig(dve.tensor_copy(cval[:, tk * D + n * 512:tk * D + (n + 1) * 512],
                                          result(8 if n + tk == 0 else 0, 512)), tile_read)
            ctx_keys(0)
            ctx_exponents(1)

            def gla_mask(n):
                dve.wait_ge(ev("gla_scores"), n + 1)
                if n >= 4:
                    dve.wait_ge(ev("gla_out"), n // 2 - 1)
                dve.tensor_tensor(att[:, n % 4 * 3 * P:(n % 4 + 1) * 3 * P], ps[n % 4][:, 0:3 * P],
                                  cst_of("mask_b" if n % 2 else "mask_f"), ALU.mult).then_inc(ev("gla_masked"), 1)

            for n in range(4):
                gla_mask(n)
            ctx_keys(1)
            ctx_state(0)
            ctx_state(1)
            lo(3)
            for hd in range(GH):
                if hd + 2 < GH:
                    gla_mask(2 * hd + 4)
                    gla_mask(2 * hd + 5)
                reciprocal_root(rstd)
                for vc in range(2):
                    k = 2 * hd + vc
                    tmp = at(zm, vc)
                    ins = dve.scalar_tensor_tensor(out=tmp, in0=ps[5 + hd % 3][:, vc * T:(vc + 1) * T],
                                                   scalar=col("g_head", k), in1=rstd[:, :], op0=ALU.mult, op1=ALU.mult)
                    if vc == 1:
                        ins.then_inc(ev("gla_read"), 1)
                        dve.wait_ge(ev("gla_read"), hd + 1)
                    else:
                        link(ins)
                    dve.wait_ge(ev("rsil_ready"), 1)
                    c.sig(dve.tensor_tensor(at(rsil, k), at(rsil, k), tmp, ALU.mult), y_f32)
                for vc in range(2):
                    k = 2 * hd + vc
                    c.take(yhi_ready)
                    c.sig(dve.tensor_tensor(at(zlo, k), at(rsil, k), at(zhi, k), ALU.subtract), y_ready)
            resid(1, None, gate=2 * DC)
            reciprocal_root(rstd)
            modulated(h, DC, 3 * DC, xlo)
            with c.loop(MC // 4, {hi_ready: 4, "unit": 4, tile_read: 4, y_f32: 4, yhi_ready: 4,
                                  y_ready: 4}) as i:
                def inner_lo(j):
                    c.take(yhi_ready)
                    c.sig(dve.tensor_tensor(at(mlo, i * 4 + j), at(ms, j), at(mhi, i * 4 + j), ALU.subtract), y_ready)

                for j in range(4):
                    c.take(tile_read)
                    c.sig(dve.tensor_tensor(at(ms, j), at(mr, j), at(mr, j), ALU.mult), y_f32)
                    if j:
                        inner_lo(j - 1)
                    lo()
                inner_lo(3)
            c.n["pe_units"] += MC
            clear_sum()

            def mlp_down(first):
                for m in range(2):
                    lo(4)
                    c.take(pe_units, 4)
                    hm = at(h, first + m)
                    c.sig(dve.scalar_tensor_tensor(out=hm, in0=ps[m][:, 0:T],
                                                   scalar=mod[:, 5 * DC + first + m:5 * DC + first + m + 1]
                                                   if isinstance(first, int) else mod[:, bass.ds(first + (5 * DC + m), 1)],
                                                   in1=hm, op0=ALU.mult, op1=ALU.add), tile_read)
                    add_square(m)

            with c.loop(DC // 2 - 1, {hi_ready: 8, "unit": 8, pe_units: 8, tile_read: 2, sq_ready: 2,
                                      ssum_ready: 2}) as i:
                mlp_down(i * 2)
            mlp_down(DC - 2)
            reciprocal_root(rstd)
            for k in range(DC):
                dve.scalar_tensor_tensor(out=at(h, k), in0=at(h, k), scalar=col("g_fin2", k), in1=rstd[:, :],
                                         op0=ALU.mult, op1=ALU.mult).then_inc(ev("out_chunk"), 1)


def columns(v, n):
    return v.reshape(n, P).T


def feature_major(x):
    return x.T.reshape(DC, P, T).transpose(1, 0, 2).reshape(P, DC * T)


def tiles(w, order=None, pad=0):
    K, M = w.shape[0] // P, w.shape[1] // P
    b = w.reshape(K, P, M, P).transpose(2, 0, 1, 3)
    if order is not None:
        b = b[order]
    if pad:
        b = np.concatenate([b, np.zeros((M, pad, P, P), w.dtype)], 1)
    return b.reshape(-1, P, P)


def wide(w):
    K, M = w.shape[0] // P, w.shape[1] // 512
    return w.reshape(K, P, M, 4, P).transpose(2, 0, 3, 1, 4).reshape(-1, P, P)


def lay_out(a):
    gu = np.stack([np.arange(FC), FC + np.arange(FC)], 1).reshape(-1)
    chb = np.stack([DC + np.arange(DC), 2 * DC + np.arange(DC), np.arange(DC)], 1).reshape(-1)
    dkv = a["w_dkv"]
    rot = dkv[:, 256:320]
    swap = np.concatenate([rot[:, 32:], rot[:, :32]], 1)
    dkv = np.concatenate([dkv[:, :256], rot, rot, swap, swap], 1)
    ukv = a["w_ukv"].reshape(256, HEADS, 2, P)
    uq = a["b_w_uq"][0].reshape(512, HEADS, 192)
    qrot = uq[:, :, 128:]
    qswap = np.concatenate([qrot[..., 32:], qrot[..., :32]], -1)
    q_pairs = np.stack([qrot.reshape(512, HP, P), qswap.reshape(512, HP, P)], 2).reshape(512, 2 * HP * P)
    win = a["gla_w_in_2"][0]
    gla = {"q": win[:, 0:512], "k": win[:, 512:1024], "v": win[:, 1024:2048], "r": win[:, 2048:3072]}
    parts = [
        tiles(a["a_w_in"][0], chb), tiles(a["a_w_out"][0]),
        tiles(a["ffn_w_up"][0], gu), tiles(a["ffn_w_down"][0], pad=2),
        tiles(dkv), tiles(a["b_w_dq"][0]),
        tiles(np.ascontiguousarray(ukv[:, :, 0]).reshape(256, D)),
        ukv[:, :, 1].reshape(2, P, 8, P).transpose(0, 2, 1, 3).reshape(-1, P, P),
        tiles(np.ascontiguousarray(uq[:, :, :128]).reshape(512, D)), tiles(q_pairs),
        tiles(a["b_w_o"][0]), tiles(a["ffn_w_up"][1], gu), tiles(a["ffn_w_down"][1], pad=2),
        tiles(gla["q"]), tiles(gla["k"]), wide(gla["v"]), tiles(gla["r"]),
        tiles(gla["k"]), wide(gla["v"]),
        tiles(a["gla_w_o_2"][0]), tiles(a["mlp_w1_2"][0]), tiles(a["mlp_w2_2"][0]),
    ]
    blocks = np.concatenate(parts)
    stream = np.ascontiguousarray(blocks.reshape(UNITS, BLK, P, P).transpose(0, 2, 1, 3)).reshape(UNITS, P, D)

    def conv(w, order):
        n = w.shape[1] // P
        return w.reshape(3, n, P)[:, order].transpose(2, 1, 0).reshape(P, 3 * n)

    vec = np.concatenate([
        columns(a["a_mix_norm"][0], 8), columns(a["ffn_norm"][0], 8), columns(a["kv_in_norm"], 8),
        columns(a["b_mix_norm"][0], 8), columns(a["b_q_norm"][0], 4), columns(a["kv_norm"], 2),
        columns(a["ffn_norm"][1], 8), columns(a["final_norm"], 8), columns(a["norm1_g_2"][0], 8),
        columns(a["norm2_g_2"][0], 8), columns(a["final_g_2"], 8), columns(a["gla_g_head_2"][0].reshape(-1), 8),
        columns(a["gla_b_a_2"][0].reshape(-1), 8), columns(a["ada_b_2"][0], 48), columns(a["c_2"][0], 8),
        columns(a["c_ctx_2"], 8), conv(a["a_conv"][0], np.arange(DC)), conv(a["ffn_conv"][0], gu),
        conv(a["ffn_conv"][1], gu)], 1)

    row, colm = np.arange(P)[:, None], np.arange(P)[None, :]
    one = np.ones((P, P), np.float32)
    hidden = np.where(colm <= row, 0.0, -1e30)
    upper, lower = (row <= colm) * one, (row >= colm) * one
    cst = np.concatenate([one, np.eye(P), upper, one, upper, lower, one, lower], 1).astype(np.float32)
    inv = (1.0 / (np.float32(10000.0) ** (np.arange(0, 64, 2, dtype=np.float32) / np.float32(64)))).astype(np.float32)
    ang = (np.arange(T, dtype=np.float32)[None, :] * inv[:, None]).astype(np.float32)
    cos = np.concatenate([np.cos(ang)] * 2)
    sin = np.concatenate([-np.sin(ang), np.sin(ang)])
    none = np.zeros((64, T), np.float32)
    rotary = np.concatenate([hidden, 0 * one, hidden] + [np.concatenate(p) for p in (
        (cos, cos), (sin, sin), (cos, none), (sin, none), (none, cos), (none, sin))], 1).astype(np.float32)

    wa1 = np.concatenate(list(a["gla_w_a1_2"][0]), 1).reshape(DC, P, 32).transpose(1, 0, 2).reshape(P, DC * 32)
    w2 = a["gla_w_a2_2"][0]
    wa2 = np.zeros((32, D), w2.dtype)
    wa2[0:16, 0:512], wa2[16:32, 512:1024] = w2[0], w2[1]
    ada = a["ada_w_2"][0].reshape(DC, P, 6, D).transpose(2, 0, 1, 3).reshape(6 * DC, P, D)
    return {"stream": stream, "xT": feature_major(a["x"][0]), "ctxT": feature_major(a["ctx_2"][0]), "vec": vec,
            "cst": cst, "rot": rotary, "wa1": wa1, "wa2": wa2, "ada": ada}


def kernel(**inputs):
    import concourse.bacc as bacc
    from concourse.bass_utils import run_bass_kernel_spmd

    arrays = {k: np.ascontiguousarray(v) for k, v in lay_out({k: np.asarray(v) for k, v in inputs.items()}).items()}
    nc = bacc.Bacc("TRN2", target_bir_lowering=False, num_devices=1)
    args = [nc.dram_tensor(k, v.shape, F32, kind="ExternalInput").ap() for k, v in arrays.items()]
    out = nc.dram_tensor("out", (P, DC * T), F32, kind="ExternalOutput").ap()
    program(nc, *args, out)
    got = run_bass_kernel_spmd(nc, [arrays], core_ids=[0]).results[0]["out"]
    return got.reshape(P, DC, T).transpose(1, 0, 2).reshape(D, T).T.reshape(1, T, D)
```
